# Optimizing a Trainium2 kernel written in Bass

```python
import numpy as np
import jax
import jax.numpy as jnp
from jax import lax

D_MODEL = 1024
BATCH = 1
SEQ = 256
DEPTH = 2

GRID_W = 64
CTX_LEN = 256
D_MIX = D_MODEL
GROUP_W = D_MIX // 4
GLA_HEADS = 4
GLA_DV = GROUP_W // GLA_HEADS
GLA_DK = GLA_DV // 2
GLA_QK_W = GLA_HEADS * GLA_DK
GLA_GATE_RANK = 16
GLA_GATE_NORM = 16.0
GLA_CHUNK = 64
CONF_WIDTH = 31
SC_WIDTH = 3
POOL_WINDOWS = (2, 4, 8, 16)
POOL_GROUPS = 4
POOL_GW = GROUP_W // POOL_GROUPS
N_GROUPS = 4
EXPERTS_PER_GROUP = 8
N_EXPERTS = N_GROUPS * EXPERTS_PER_GROUP
TOP_K_INNER = 2
D_EXPERT = D_MODEL // 2
MOE_BLOCK = 256
NORM_EPS = 1e-6
IN_SPLITS = (GLA_QK_W, GLA_QK_W, GROUP_W, GROUP_W, GLA_GATE_RANK, GLA_GATE_RANK,
             2 * GROUP_W, GROUP_W, GROUP_W, GROUP_W, GROUP_W)
N_IN = 2 * GLA_QK_W + 2 * GLA_GATE_RANK + 8 * GROUP_W

kernel_name = 'hybrid_parallel_group_flow_block'

def rms_norm(x, g):
    xf = x.astype(jnp.float32)
    y = xf * lax.rsqrt(jnp.mean(xf * xf, axis=-1, keepdims=True) + NORM_EPS)
    return (y * g.astype(jnp.float32)).astype(x.dtype)

def layer_norm(x, g, b):
    xf = x.astype(jnp.float32)
    xc = xf - jnp.mean(xf, axis=-1, keepdims=True)
    y = xc * lax.rsqrt(jnp.mean(xc * xc, axis=-1, keepdims=True) + NORM_EPS)
    return (y * g.astype(jnp.float32) + b.astype(jnp.float32)).astype(x.dtype)

def adaln(cvec, w, b):
    m = jax.nn.silu(cvec) @ w + b
    m = m.reshape(m.shape[:-1] + (6, D_MODEL))
    return [m[..., None, i, :] for i in range(6)]

def modulate(x, shift, scale):
    return x * (1 + scale) + shift

def split_columns(h):
    idx = np.cumsum(IN_SPLITS)[:-1].tolist()
    return jnp.split(h, idx, axis=-1)

def dwconv(x, w):
    k = w.shape[0]
    return lax.conv_general_dilated(
        x, w[:, None, :].astype(x.dtype), window_strides=(1,), padding=[(k // 2, k // 2)],
        dimension_numbers=('NWC', 'WIO', 'NWC'), feature_group_count=x.shape[-1])

def axial_dwconv(x, w):
    bsz, length, ch = x.shape
    rows = length // GRID_W
    half = ch // 2
    g = x.reshape(bsz, rows, GRID_W, ch)
    horiz = dwconv(g[..., :half].reshape(bsz * rows, GRID_W, half), w[:, :half])
    horiz = horiz.reshape(bsz, rows, GRID_W, half)
    vert = g[..., half:].transpose(0, 2, 1, 3).reshape(bsz * GRID_W, rows, ch - half)
    vert = dwconv(vert, w[:, half:]).reshape(bsz, GRID_W, rows, ch - half).transpose(0, 2, 1, 3)
    return jnp.concatenate([horiz, vert], axis=-1).reshape(bsz, length, ch)

def centred_mean(x, win):
    length = x.shape[1]
    cs = jnp.pad(jnp.cumsum(x.astype(jnp.float32), axis=1), ((0, 0), (1, 0), (0, 0)))
    t = np.arange(length)
    lo = np.clip(t - win // 2, 0, length)
    hi = np.clip(t + win // 2, 0, length)
    cnt = jnp.asarray((hi - lo)[None, :, None], jnp.float32)
    return ((cs[:, hi] - cs[:, lo]) / cnt).astype(x.dtype)

def row_mean(x, win):
    bsz, length, ch = x.shape
    rows = length // GRID_W
    return centred_mean(x.reshape(bsz * rows, GRID_W, ch), win).reshape(bsz, length, ch)

def to_heads(t, n_heads):
    bsz, length, width = t.shape
    return t.reshape(bsz, length, n_heads, width // n_heads).transpose(0, 2, 1, 3).astype(jnp.float32)

def gla_chunked(q, k, v, log_a, s0):
    bsz, nh, length, dk = q.shape
    dv = v.shape[-1]
    nc = length // GLA_CHUNK
    shp = (bsz, nh, nc, GLA_CHUNK)
    q, k, log_a = (t.reshape(shp + (dk,)) for t in (q, k, log_a))
    v = v.reshape(shp + (dv,))
    b = jnp.cumsum(log_a, axis=3)
    b_last = b[:, :, :, -1:, :]
    q_dec = q * jnp.exp(b)
    k_inv = k * jnp.exp(-b)
    mask = np.tril(np.ones((GLA_CHUNK, GLA_CHUNK), dtype=bool))
    scores = jnp.where(mask, jnp.einsum('bhnid,bhnjd->bhnij', q_dec, k_inv), 0.0)
    o_intra = jnp.einsum('bhnij,bhnjv->bhniv', scores, v)
    chunk_kv = jnp.einsum('bhnjd,bhnjv->bhndv', k * jnp.exp(b_last - b), v)
    chunk_decay = jnp.exp(b_last[:, :, :, 0, :])

    def step(state, inp):
        dec, kv = inp
        return dec[..., None] * state + kv, state

    s_final, s_in = lax.scan(step, s0, (jnp.moveaxis(chunk_decay, 2, 0), jnp.moveaxis(chunk_kv, 2, 0)))
    o_inter = jnp.einsum('bhnid,nbhdv->bhniv', q_dec, s_in)
    return (o_intra + o_inter).reshape(bsz, nh, length, dv), s_final

def gla_bidir(q, k, v, la_f, la_b, s0_f, s0_b):
    o_f, s_f = gla_chunked(q, k, v, la_f, s0_f)
    rev = lambda t: jnp.flip(t, axis=2)
    o_b, s_b = gla_chunked(rev(q), rev(k), rev(v), rev(la_b), s0_b)
    return o_f + rev(o_b), s_f, s_b

def gla_branch(cols, w_gf, b_gf, w_gb, b_gb, g_out, s0_f, s0_b):
    q, k, v, g, z_f, z_b = cols[:6]

    def decay(z, w, b):
        return to_heads(jax.nn.log_sigmoid((z @ w + b).astype(jnp.float32)) / GLA_GATE_NORM, GLA_HEADS)

    o, s_f, s_b = gla_bidir(to_heads(q, GLA_HEADS) * GLA_DK ** -0.5, to_heads(k, GLA_HEADS),
                            to_heads(v, GLA_HEADS), decay(z_f, w_gf, b_gf), decay(z_b, w_gb, b_gb),
                            s0_f, s0_b)
    o = o * lax.rsqrt(jnp.mean(o * o, axis=-1, keepdims=True) + NORM_EPS)
    bsz, nh, length, dv = o.shape
    o = o.transpose(0, 2, 1, 3).reshape(bsz, length, nh * dv) * g_out.astype(jnp.float32)
    return (o * jax.nn.silu(g.astype(jnp.float32))).astype(g.dtype), s_f, s_b

def local_branches(cols, conf_w, conf_b, conf_g, conf_beta, sc_w, pool_w, pool_scale, conv_fn, mean_fn):
    conf_in, sc_b, sc_c, sc_x, pool_in = cols[6:]
    a, gate = jnp.split(conf_in, 2, axis=-1)
    u = conv_fn(a * jax.nn.sigmoid(gate), conf_w) + conf_b
    y_conf = jax.nn.silu(layer_norm(u, conf_g, conf_beta))
    y_sc = sc_b * conv_fn(sc_c * sc_x, sc_w)
    diffs = []
    for i, win in enumerate(POOL_WINDOWS):
        hg = pool_in[..., i * POOL_GW:(i + 1) * POOL_GW]
        diffs.append(mean_fn(hg, win) - hg)
    y_pool = jnp.einsum('blgc,gcd->blgd', jnp.stack(diffs, axis=-2), pool_w).reshape(pool_in.shape) * pool_scale
    return jnp.concatenate([y_conf, y_sc, y_pool], axis=-1)

def grouped_experts(h, eid, gate, w_in, w_out):
    n, d = h.shape
    a = eid.shape[0]
    tok = jnp.arange(a) // TOP_K_INNER
    order = jnp.argsort(eid)
    e_s, tok_s, g_s = eid[order], tok[order], gate[order]
    counts = jnp.zeros((N_EXPERTS,), jnp.int32).at[eid].add(1)
    starts = jnp.cumsum(counts) - counts
    padded = (counts + MOE_BLOCK - 1) // MOE_BLOCK * MOE_BLOCK
    pad_end = jnp.cumsum(padded)
    pad_start = pad_end - padded
    dest = pad_start[e_s] + jnp.arange(a) - starts[e_s]
    n_blocks = -(-a // MOE_BLOCK) + N_EXPERTS
    slots = n_blocks * MOE_BLOCK
    slot_tok = jnp.zeros((slots,), jnp.int32).at[dest].set(tok_s)
    slot_gate = jnp.zeros((slots,), gate.dtype).at[dest].set(g_s)
    blk_expert = jnp.minimum(jnp.searchsorted(pad_end, jnp.arange(n_blocks) * MOE_BLOCK, side='right'),
                             N_EXPERTS - 1)

    def run_block(args):
        e, toks = args
        xb = h[toks]
        gt, up = jnp.split(xb @ w_in[e], 2, axis=-1)
        return (jax.nn.silu(gt) * up) @ w_out[e]

    y = lax.map(run_block, (blk_expert, slot_tok.reshape(n_blocks, MOE_BLOCK)))
    y = y.reshape(slots, d) * slot_gate[:, None].astype(y.dtype)
    return jax.ops.segment_sum(y, slot_tok, num_segments=n)

def hier_moe(h, w_rg, b_rg, w_re, b_re, w_e_in, w_e_out):
    n = h.shape[0]
    rows = jnp.arange(n)
    lg = (h @ w_rg + b_rg).astype(jnp.float32)
    grp = jnp.argmax(lg, axis=-1)
    p_grp = jax.nn.softmax(lg, axis=-1)[rows, grp][:, None]
    le = (h @ w_re + b_re).astype(jnp.float32).reshape(n, N_GROUPS, EXPERTS_PER_GROUP)
    top_v, top_i = lax.top_k(le[rows, grp], TOP_K_INNER)
    w = jax.nn.softmax(top_v, axis=-1) * p_grp
    eid = grp[:, None] * EXPERTS_PER_GROUP + top_i
    return grouped_experts(h, eid.reshape(-1), w.reshape(-1), w_e_in, w_e_out)

def setup_inputs(seed: int = 0) -> dict:
    key = jax.random.key(seed)
    keys = iter(jax.random.split(key, 32))

    def rnd(shape, scale):
        return jax.random.normal(next(keys), shape, jnp.float32) * scale

    L, D = DEPTH, D_MODEL
    return {
        'x': rnd((BATCH, SEQ, D), 1.0),
        'c': rnd((BATCH, D), 1.0),
        'ctx': rnd((BATCH, CTX_LEN, D), 1.0),
        'c_ctx': rnd((D,), 1.0),
        'w_mod': rnd((L, D, 6 * D), 0.5 * D ** -0.5),
        'b_mod': rnd((L, 6 * D), 0.02),
        'g_norm1': 1.0 + rnd((L, D), 0.05),
        'g_norm2': 1.0 + rnd((L, D), 0.05),
        'w_in': rnd((L, D, N_IN), D ** -0.5),
        'gla_w_gate_f': rnd((L, GLA_GATE_RANK, GLA_QK_W), GLA_GATE_RANK ** -0.5),
        'gla_b_gate_f': rnd((L, GLA_QK_W), 0.1),
        'gla_w_gate_b': rnd((L, GLA_GATE_RANK, GLA_QK_W), GLA_GATE_RANK ** -0.5),
        'gla_b_gate_b': rnd((L, GLA_QK_W), 0.1),
        'gla_g_out': 1.0 + rnd((L, GROUP_W), 0.05),
        'conf_w_dw': rnd((L, CONF_WIDTH, GROUP_W), CONF_WIDTH ** -0.5),
        'conf_b_dw': rnd((L, GROUP_W), 0.02),
        'conf_ln_g': 1.0 + rnd((L, GROUP_W), 0.05),
        'conf_ln_b': rnd((L, GROUP_W), 0.02),
        'sc_w_dw': rnd((L, SC_WIDTH, GROUP_W), SC_WIDTH ** -0.5),
        'pool_w': rnd((L, POOL_GROUPS, POOL_GW, POOL_GW), POOL_GW ** -0.5),
        'pool_scale': 1.0 + rnd((L, GROUP_W), 0.1),
        'w_out': rnd((L, D_MIX, D), D_MIX ** -0.5),
        'router_w_group': rnd((L, D, N_GROUPS), D ** -0.5),
        'router_b_group': rnd((L, N_GROUPS), 0.01),
        'router_w_expert': rnd((L, D, N_EXPERTS), D ** -0.5),
        'router_b_expert': rnd((L, N_EXPERTS), 0.01),
        'expert_w_in': rnd((L, N_EXPERTS, D, 2 * D_EXPERT), D ** -0.5),
        'expert_w_out': rnd((L, N_EXPERTS, D_EXPERT, D), D_EXPERT ** -0.5),
        'g_final': 1.0 + rnd((D,), 0.05),
    }

def reference(x, c, ctx, c_ctx, w_mod, b_mod, g_norm1, g_norm2, w_in, gla_w_gate_f, gla_b_gate_f,
              gla_w_gate_b, gla_b_gate_b, gla_g_out, conf_w_dw, conf_b_dw, conf_ln_g, conf_ln_b,
              sc_w_dw, pool_w, pool_scale, w_out, router_w_group, router_b_group, router_w_expert,
              router_b_expert, expert_w_in, expert_w_out, g_final):
    bsz, seq, d = x.shape
    n_lat = bsz * seq
    s0 = jnp.zeros((bsz, GLA_HEADS, GLA_DK, GLA_DV), jnp.float32)
    for l in range(DEPTH):
        last = l == DEPTH - 1
        sh1, sc1, ga1, sh2, sc2, ga2 = adaln(c, w_mod[l], b_mod[l])
        csh1, csc1, cga1, csh2, csc2, cga2 = adaln(c_ctx, w_mod[l], b_mod[l])
        gla_p = (gla_w_gate_f[l], gla_b_gate_f[l], gla_w_gate_b[l], gla_b_gate_b[l], gla_g_out[l])
        loc_p = (conf_w_dw[l], conf_b_dw[l], conf_ln_g[l], conf_ln_b[l], sc_w_dw[l], pool_w[l], pool_scale[l])
        moe_p = (router_w_group[l], router_b_group[l], router_w_expert[l], router_b_expert[l],
                 expert_w_in[l], expert_w_out[l])

        cols_c = split_columns(modulate(rms_norm(ctx, g_norm1[l]), csh1, csc1) @ w_in[l])
        cols_x = split_columns(modulate(rms_norm(x, g_norm1[l]), sh1, sc1) @ w_in[l])
        y_gla_c, s_f, s_b = gla_branch(cols_c, *gla_p, s0, s0)
        y_gla_x, _, _ = gla_branch(cols_x, *gla_p, s_f, s_b)
        y_loc_x = local_branches(cols_x, *loc_p, axial_dwconv, row_mean)
        x = x + ga1 * (jnp.concatenate([y_gla_x, y_loc_x], axis=-1) @ w_out[l])
        if not last:
            y_loc_c = local_branches(cols_c, *loc_p, dwconv, centred_mean)
            ctx = ctx + cga1 * (jnp.concatenate([y_gla_c, y_loc_c], axis=-1) @ w_out[l])

        m_x = modulate(rms_norm(x, g_norm2[l]), sh2, sc2).reshape(n_lat, d)
        if last:
            x = x + ga2 * hier_moe(m_x, *moe_p).reshape(bsz, seq, d)
        else:
            m_c = modulate(rms_norm(ctx, g_norm2[l]), csh2, csc2).reshape(-1, d)
            y = hier_moe(jnp.concatenate([m_x, m_c], axis=0), *moe_p)
            x = x + ga2 * y[:n_lat].reshape(bsz, seq, d)
            ctx = ctx + cga2 * y[n_lat:].reshape(ctx.shape)
    return rms_norm(x, g_final)


_drawn_inputs = setup_inputs


def setup_inputs(seed=0):
    import zlib

    import numpy as np

    out = dict(_drawn_inputs(seed))
    spreads = {}
    factors = {'c_ctx': 2.983,
     'gla_w_gate_f': 2.752,
     'gla_b_gate_f': 5.475,
     'gla_w_gate_b': 3.403,
     'gla_b_gate_b': 8.0,
     'gla_g_out': 5.184,
     'conf_b_dw': 5.134,
     'conf_ln_g': 5.796,
     'conf_ln_b': 21.34,
     'router_b_group': 14.404,
     'router_b_expert': 21.91,
     'pool_scale': 3.177}
    for name, (base, spread) in spreads.items():
        noise = np.random.default_rng([zlib.crc32(name.encode()), seed]).standard_normal(out[name].shape)
        drawn = base * np.exp(spread * noise) if base else spread * noise
        out[name] = jnp.asarray(drawn.astype(out[name].dtype))
    for name, factor in factors.items():
        out[name] = (out[name] * factor).astype(out[name].dtype)
    return out
```

```python
import numpy as np
from contextlib import ExitStack

import concourse.bass as bass
from concourse import mybir

ALU = mybir.AluOpType
ACT = mybir.ActivationFunctionType
F32 = mybir.dt.float32
BF16 = mybir.dt.bfloat16
I32 = mybir.dt.int32
U32 = mybir.dt.uint32
AX_X = mybir.AxisListType.X

P = 128
D = 1024
KT = D // P
DEPTH = 2
SEQ = 256
CTX = 256
XT_TILES = SEQ // P
TILES = (SEQ + CTX) // P
GRID_W = 64
ROWS = SEQ // GRID_W
GROUP_W = D // 4
HEADS = 4
DV = GROUP_W // HEADS
DK = DV // 2
QK_W = HEADS * DK
RANK = 16
GATE_NORM = 16.0
CHUNK = 64
NCH = TILES * 2
CONF_K = 31
SC_K = 3
WINDOWS = (2, 4, 8, 16)
N_IN = 2 * QK_W + 2 * RANK + 8 * GROUP_W
NG = 4
EPG = 8
NE = NG * EPG
DE = D // 2
EPS = 1e-6
BIG = 1.0e30
BUFS = 4
AHEAD = BUFS - 1
BLK = 64
HALF = D // 2
VEC_ROWS = CONF_K + 3 + SC_K + 1
V_CB, V_LG, V_LB, V_SC, V_PS = CONF_K, CONF_K + 1, CONF_K + 2, CONF_K + 3, CONF_K + 3 + SC_K

C_Q, C_G, C_Z = 0, 2 * QK_W + GROUP_W, 2 * QK_W + 2 * GROUP_W
C_CONF = C_Z + 2 * RANK
C_SC = C_CONF + 2 * GROUP_W
C_XP = C_SC + 2 * GROUP_W
PADW = 8
PX = GRID_W + 2 * PADW
POOL_X = ROWS * PX
POOL_N = POOL_X + CTX + 2 * PADW


def layer_tiles(l):
    return XT_TILES if l == DEPTH - 1 else TILES


CONST_COLS = {}


def _const_layout():
    at = 0
    for name, n in (("ident", P), ("ones", P), ("before", P), ("cum_f", P), ("cum_b", P), ("after", P),
                    ("prev", P), ("sel_x", P), ("sel_c", P), ("sel", 2), ("heads", HEADS), ("eps", 1), ("chunks", 2),
                    ("tok1", 1), ("half", 1), ("rev4", NG), ("rev32", NE), ("thr", 8),
                    ("hi0", 2 * TILES), ("hi1", 2 * XT_TILES), ("inv", 2 * POOL_N)):
        CONST_COLS[name] = (at, n)
        at += n
    return at


CONST_N = _const_layout()


def constants():
    c = np.zeros((P, CONST_N), np.float32)

    def put(name, v):
        a, n = CONST_COLS[name]
        c[:, a:a + n] = v

    j, i = np.arange(P)[:, None], np.arange(P)[None, :]
    same = (j // CHUNK) == (i // CHUNK)
    put("ident", j == i)
    put("ones", 1.0)
    put("before", j < i)
    put("cum_f", same & (j <= i))
    put("cum_b", same & (j >= i))
    put("after", same & (j > i))
    put("prev", same & (j < i))
    put("sel_x", (j % 32) == 0)
    put("sel_c", (j % 32) == 1)
    put("sel", (j % 32) == np.arange(2)[None, :])
    put("heads", (j // DK) == np.arange(HEADS)[None, :])
    put("eps", EPS)
    put("chunks", (j // CHUNK) == np.arange(2)[None, :])
    put("tok1", j + 1)
    put("half", j // BLK)
    put("rev4", NG - np.arange(NG)[None, :])
    put("rev32", NE - np.arange(NE)[None, :])
    put("thr", BLK * (1 + np.arange(8))[None, :])
    for l in range(2):
        nt = layer_tiles(l)
        put(f"hi{l}", np.array([cj * nt * P + t * P for cj in range(2) for t in range(nt)])[None, :])
    inv = np.zeros((P, 2, POOL_N), np.float32)

    def counts(length, win):
        t = np.arange(length)
        return np.clip(t + win // 2, 0, length) - np.clip(t - win // 2, 0, length)

    for g, win in enumerate(WINDOWS):
        parts = slice(64 * (g % 2), 64 * (g % 2) + 64)
        for r in range(ROWS):
            inv[parts, g // 2, r * PX + PADW:r * PX + PADW + GRID_W] = 1.0 / counts(GRID_W, win)
        inv[parts, g // 2, POOL_X + PADW:POOL_X + PADW + CTX] = 1.0 / counts(CTX, win)
    put("inv", inv.reshape(P, -1))
    return c


def psum_jobs(l):
    nt = layer_tiles(l)
    vs = 2 if l < DEPTH - 1 else 1
    jobs = [(("vec",), "D")]

    def mod(i, gate):
        out = [(("mod", 2 * i), "A"), (("mod", 2 * i + 1), "A")]
        if gate:
            return [(("mod", 2 * i), "A")] + [(("gate", i, 0, v), "D") for v in range(vs)] + \
                   [(("mod", 2 * i + 1), "A")] + [(("gate", i, 1, v), "D") for v in range(vs)]
        return out + [(("modT", i), "D")]

    jobs += mod(0, False) + mod(1, False)
    jobs += [(("norm", 0, k), "AD"[k % 2]) for k in range(KT)]
    jobs += [(("cgate", 0), "A"), (("ca", 0), "D"), (("cgate", 1), "A"), (("ca", 1), "D")]
    jobs += [(("scb", 0), "A"), (("scb", 1), "A"), (("scc", 0), "A"), (("scc", 1), "A")]
    jobs += [(("scx", 0), "D"), (("scx", 1), "D"), (("pool", 0), "A"), (("pool", 1), "A")]
    jobs += [(("qkv", t), "A") for t in range(TILES)]
    jobs += [(("z",), "A")]
    jobs += [(("zw", 0), "AD"), (("zw", 1), "AD")]
    jobs += [(("g", t), "A") for t in range(nt)]
    jobs += mod(3, False) + mod(4, False) + mod(2, True)
    jobs += [(("mean",), "D"), (("var",), "A")]
    jobs += [(("cum", i), "A") for i in range(4)] + [(("dec",), "A")]
    jobs += [(("pm", 0), "D"), (("pm", 1), "D")]
    jobs += [(("tq", 0), "A"), (("tk", 0), "A"), (("tq", 1), "A"), (("tk", 1), "A")]
    jobs += [(("kv", t, par), "D") for t in (2, 3, 0, 1) for par in range(2)]
    for t in range(nt):
        jobs += [(("score", t, 0), "D"), (("score", t, 1), "D"), (("o", t), "AD")]
        if t:
            jobs += [(("ty", t - 1), "A")]
    jobs += [(("ty", nt - 1), "A")]
    jobs += [(("out", t, h), "D") for t in range(nt) for h in range(2)]
    jobs += mod(5, True)
    jobs += [(("norm", 1, k), "AD"[k % 2]) for k in range(KT)]
    jobs += [(("router",), "A"), (("routerT",), "D")]
    jobs += [(("htok", t, h), "AD"[h]) for t in range(nt) for h in range(2)]
    jobs += [(("pos",), "D"), (("cnt",), "D"), (("slots",), "D"), (("extra",), "D")]
    return [((l,) + k, c) for k, c in jobs]


class PsumJobs:

    def __init__(self, jobs):
        self.keys = [k for k, _ in jobs]
        self.readers = [c for _, c in jobs]
        self.at = {k: i for i, k in enumerate(self.keys)}
        self.taken = {"A": [], "D": []}
        self.upto = []
        n = {"A": 0, "D": 0}
        for c in self.readers:
            for x in c:
                n[x] += 1
            self.upto.append(dict(n))
        self.next = 0

    def bank(self, *key):
        return self.at[key] % 8


class Ring:

    def __init__(self):
        self.plan = []
        self.count = [0] * 6
        self.where = {}

    def add(self, key, slot):
        self.count[slot] += 16
        self.where[key] = (slot, self.count[slot])
        self.plan.append(key)


def stream(l):
    first = [(l, "mod", n) for n in range(4)] + [(l, "win", n) for n in range(5)]
    return first + [(l, "mod", n) for n in (6, 7, 8, 9, 4, 5)] + [(l, "wout", 0), (l, "wout", 1)] + \
        [(l, "mod", n) for n in (10, 11)]


def build(nc, t_in, out):
    ctx = ExitStack()
    with ctx:
        def sb(name, shape, dt=F32):
            return ctx.enter_context(nc.sbuf_tensor(name, shape, dt))

        def sem(name):
            return ctx.enter_context(nc.semaphore(name))

        SLOT = 4 * D
        ring = sb("ring", [P, 6 * SLOT])
        X = sb("resid", [P, TILES, D])
        gates = sb("gates", [P, 2, D])
        actT = sb("actT", [P, KT * TILES * P])
        work = sb("work", [P, 6144])
        states = sb("states", [P, 2 * NCH * 256 + 256])
        zT = sb("zT", [P, TILES * P])
        cst = sb("cst", [P, CONST_N])
        wgate = sb("wgate", [P, 256])
        gout = sb("gout", [P, GROUP_W])
        vecs = sb("vecs", [P, GROUP_W])
        chv = sb("chv", [P, 2, VEC_ROWS])
        poolw = sb("poolw", [P, 2, P])
        wre = sb("wre", [P, KT, NE])
        wrg = sb("wrg", [P, KT, NG])
        wrt = sb("wrt", [P, KT, NE + NG])
        rbias = sb("rbias", [P, 1])
        gnorm = sb("gnorm", [P, 2, KT])
        bmod = sb("bmod", [P, 6, KT])
        modv = sb("modv", [P, 2, 2, 2, KT])
        msb = sb("msb", [P, 2, 512])
        csil = sb("csil", [P, KT, 32])
        craw = sb("craw", [P, 2, KT])
        small = sb("small", [P, 600])
        gtab = sb("gtab", [P, 8, NE + AHEAD], I32)
        stab = sb("stab", [P, 8, NE + AHEAD], I32)
        xtab = sb("xtab", [1, 2 * NE], I32)
        gidx = sb("gidx", [P, BUFS], U32)
        sidx = sb("sidx", [P, BUFS], U32)
        spare = sb("spare", [P, BUFS])
        gidx_x = sb("gidx_x", [P, 1], U32)
        sidx_x = sb("sidx_x", [P, 1], U32)

        PS = [ctx.enter_context(nc.psum_tensor(f"bank{i}", [P, 512], F32)) for i in range(8)]
        hd = nc.dram_tensor("h_rows", [2 * TILES * P, HALF], F32, kind="Internal").ap()
        yd = nc.dram_tensor("y_rows", [2 * 2 * TILES * P, HALF], F32, kind="Internal").ap()

        def const(name, parts=P):
            a, n = CONST_COLS[name]
            return cst[0:parts, a:a + n]

        def cut(t, a, n, dt=None):
            v = t[:, a:a + n]
            return v if dt is None else v.bitcast(dt)

        def bc(ap, axis, n):
            v = ap.unsqueeze(axis)
            shape = list(v.shape)
            shape[axis] = n
            return v.broadcast_to(shape)

        ident = const("ident")
        ones = const("ones")
        slot = [ring[:, s * SLOT:(s + 1) * SLOT] for s in range(6)]
        aT = actT[:, :].rearrange("p (k t) -> p k t", k=KT)
        xn = work[:, 0:4096].rearrange("p (t d) -> p t d", t=TILES)
        qkvg = work[:, 0:3072].rearrange("p (t c) -> p t c", t=TILES)
        ex = work[:, 3072:6144].rearrange("p (i t c) -> p i t c", i=6, t=TILES)
        conv = ring[:, 4 * SLOT:6 * SLOT]
        sg = conv[:, 0:1024].rearrange("p (m t) -> p m t", m=2)
        glu = conv[:, 1024:2048].rearrange("p (m t) -> p m t", m=2)
        u = conv[:, 2048:3072].rearrange("p (m t) -> p m t", m=2)
        scb = conv[:, 3072:4096].rearrange("p (m t) -> p m t", m=2)
        scc = conv[:, 4096:5120].rearrange("p (m t) -> p m t", m=2)
        scp = conv[:, 5120:6144].rearrange("p (m t) -> p m t", m=2)
        sca = conv[:, 6144:7168].rearrange("p (m t) -> p m t", m=2)
        la = conv[:, 7168:8192].rearrange("p (i t c) -> p i t c", i=2, t=TILES)
        lab = ex[:, 0:2, :, :]
        qdT = scc.rearrange("p m t -> p (m t)").rearrange("p (m t) -> p m t", m=2)
        kiT = glu
        scm = scp
        qbd = scb
        S = states[:, 0:2 * NCH * 256].rearrange("p (i c n) -> p i c n", i=2, c=NCH)
        S0 = states[:, 2 * NCH * 256:]
        pin = states[:, 0:2 * POOL_N].rearrange("p (m n) -> p m n", m=2)
        pA = states[:, 2 * POOL_N:3 * POOL_N]
        pB = states[:, 3 * POOL_N:4 * POOL_N]
        htok = states[:, 0:4096].rearrange("p (t d) -> p t d", t=TILES)
        oneh = work[:, 4096:6144].bitcast(BF16).rearrange("p (n s) -> p n s", s=512)
        iota = work[:, 2048:2560]
        xg = work[:, 0:2048].rearrange("p (b n) -> p b n", b=BUFS)
        xeT = work[:, 2048:3072].rearrange("p (b k n) -> p b k n", b=2, k=4)
        raw = work[:, 3072:3584]
        sil = work[:, 3584:3840].rearrange("p (k n) -> p k n", k=4)
        hT = work[:, 3840:4096].rearrange("p (k n) -> p k n", k=4)
        ye = work[:, 4096:6144].rearrange("p (b n) -> p b n", b=BUFS)
        xg_x = actT[:, 0:512]
        xeT_x = actT[:, 512:1024].rearrange("p (k n) -> p k n", k=4)
        raw_x = actT[:, 1024:1536]
        sil_x = actT[:, 1536:1792].rearrange("p (k n) -> p k n", k=4)
        hT_x = actT[:, 1792:2048].rearrange("p (k n) -> p k n", k=4)
        ye_x = actT[:, 2048:2560]
        yin = states[:, 0:4096].rearrange("p (b j d) -> p b j d", b=2, j=2)
        gfin = actT[:, 2560:3584]
        sqt = actT[:, 2560:3584]

        class Small:
            at = 0

            def __call__(self, n):
                self.at += n
                assert self.at <= 600
                return small[:, self.at - n:self.at]

        sm = Small()
        ss = sm(TILES)
        rstd = sm(TILES)
        sso = sm(TILES * HEADS)
        ro = sm(TILES * HEADS)
        dec = sm(2 * NCH).rearrange("p (i c) -> p i c", i=2)
        mt = sm(2 * KT).rearrange("p (v k) -> p v k", v=2)
        logit = sm(TILES * (NE + NG)).rearrange("p (t n) -> p t n", t=TILES)
        r4 = [sm(TILES * NG).rearrange("p (t n) -> p t n", t=TILES) for _ in range(4)]
        rr = [sm(TILES) for _ in range(8)]
        wt = sm(2 * TILES).rearrange("p (j t) -> p j t", j=2)
        pos = sm(2 * TILES).rearrange("p (j t) -> p j t", j=2)
        cnt = sm(9)
        l32 = [work[:, 512 + 128 * i:640 + 128 * i].rearrange("p (t n) -> p t n", t=TILES) for i in range(6)]
        rhs = [work[:, 1280 + 128 * i:1408 + 128 * i].bitcast(BF16).rearrange("p (t n) -> p t n", t=TILES)
               for i in range(2)]
        tabf = [work[:, 2560 + 256 * i:2816 + 256 * i].rearrange("p (b e) -> p b e", b=8) for i in range(3)]
        lgT = work[:, 3328:3840]
        made, read_a, read_d = sem("made"), sem("read_a"), sem("read_d")
        slot_ready = [sem(f"slot_ready{s}") for s in range(6)]
        expert_free = sem("experts_read")
        s_in = sem("inputs_loaded")
        s_par = sem("params_loaded")
        s_gb = sem("gate_bias_loaded")
        s_dve, s_act, s_pool = sem("vector_step"), sem("scalar_step"), sem("pool_step")
        s_setup = sem("pool_zeroed")
        s_csil = sem("silu_c")
        s_modv = sem("modulation_ready")
        s_ss = sem("squares_summed")
        s_rstd = sem("rstd_ready")
        s_so, s_ro = sem("o_squares_summed"), sem("o_rstd")
        s_xn = sem("normed")
        s_pdiff = sem("pool_diff_ready")
        s_lab = sem("log1p_ready")
        s_u = sem("conf_u_ready")
        s_sq = sem("conf_squared")
        s_yc = sem("conf_rows_ready")
        s_un = sem("conf_normed")
        s_qd = sem("decayed_qk_ready")
        s_S = sem("states_ready")
        s_qbd = sem("q_by_heads")
        s_y = sem("gla_rows_ready")
        s_res = sem("residual_added")
        s_ddh = sem("exp_input_ready")
        s_eg = sem("group_exp_ready")
        s_hd = sem("h_rows_stored")
        s_M = sem("choices_ready")
        s_oneh = sem("positions_onehot")
        s_nb = sem("block_counts")
        s_iota = sem("iota_loaded")
        m_gi, m_si = sem("m_gather_index"), sem("m_scatter_index")
        m_gath = [sem(f"m_gathered{b}") for b in range(BUFS)]
        m_scat = [sem(f"m_scattered{b}") for b in range(BUFS)]
        m_t1, m_xeT, m_g1, m_raw = sem("m_transposed"), sem("m_tokens_ready"), sem("m_hidden"), sem("m_hidden_sb")
        m_t2, m_sil, m_hT, m_g2, m_y = sem("m_hidden_T"), sem("m_silu"), sem("m_act_ready"), sem("m_out"), sem("m_out_sb")
        x_names = ("indices", "gathered", "transposed", "tokens_ready", "hidden", "hidden_sb", "hidden_T", "silu",
                   "act_ready", "out", "out_sb", "scattered")
        x_idx, x_gath, x_t1, x_xeT, x_g1, x_raw, x_t2, x_sil, x_hT, x_g2, x_y, x_scat = [
            [sem(f"x_{n}{l}") for l in range(DEPTH)] for n in x_names]
        s_zx = sem("extra_total")
        s_yin = [sem("y_loaded0"), sem("y_loaded1")]
        s_mark = sem("pool_goes_on")
        s_comb = sem("combined")
        s_gf = sem("final_gain_loaded")
        s_fin = sem("final_rows")
        s_out = sem("stored")

        jobs = PsumJobs([j for l in range(DEPTH) for j in psum_jobs(l)])
        chunks = Ring()
        for l in range(DEPTH):
            for n, key in enumerate(stream(l)):
                chunks.add(key, n % 4)
            for e in range(NE):
                for c in range(3):
                    chunks.add((l, "expert", e, c), 3 * (e % 2) + c)
        N_PAR = 22
        LAYER_T = [layer_tiles(l) for l in range(DEPTH)]

        def take(eng, l, *key):
            i = jobs.at[(l,) + key]
            eng.wait_ge(made, i + 1)
            return PS[i % 8]

        def done(ins, who, l, *key):
            i = jobs.at[(l,) + key]
            jobs.taken[who].append(i)
            assert jobs.taken[who] == sorted(jobs.taken[who]) and jobs.upto[i][who] == len(jobs.taken[who]), key
            return ins.then_inc(read_a if who == "A" else read_d, 1)

        def got(eng, who, l, *key):
            eng.wait_ge(read_a if who == "A" else read_d, jobs.upto[jobs.at[(l,) + key]][who])

        def last_use(key):
            l, name, n = key
            if name == "mod":
                return key
            if name == "wout":
                return (l, "out", LAYER_T[l] - 1, 1)
            return ((l, "ca", 1), (l, "scc", 1), (l, "pool", 1), (l, "qkv", TILES - 1), (l, "g", LAYER_T[l] - 1))[n]

        wmod = [t_in["w_mod"][l].rearrange("(p k) n -> p k n", k=KT) for l in range(DEPTH)]
        win = [t_in["w_in"][l].rearrange("(p k) n -> p k n", k=KT) for l in range(DEPTH)]
        wout = [t_in["w_out"][l].rearrange("(k p) n -> p k n", p=P) for l in range(DEPTH)]
        WIN = [(C_CONF, C_SC), (C_SC, C_XP), (C_XP, N_IN), (C_Q, C_G), (C_G, C_CONF)]
        ewin = t_in["expert_w_in"].rearrange("l e (p h k) n -> (l e) h p (k n)", h=2, k=4)
        ewout = t_in["expert_w_out"].rearrange("l e (p k) n -> (l e) p (k n)", k=4)

        def slot_view(key):
            s, _ = chunks.where[key]
            v = slot[s]
            if key[1] == "mod":
                return v.rearrange("p (k n) -> p k n", k=KT)
            if key[1] == "win":
                a, b = WIN[key[2]]
                return v[:, 0:KT * (b - a)].rearrange("p (k n) -> p k n", k=KT)
            return v.rearrange("p (k n) -> p k n", k=4)

        ORDER = [[4, 5, 6, 7, 0, 1, 2, 3], [7, 6, 5, 4, 3, 2, 1, 0]]

        def state_in(d, c):
            n = ORDER[d].index(c)
            return S[:, d, ORDER[d][n - 1], :] if n else S0

        def route(dve, link, tt, ts, stt, l, nt):
            N = nt * P
            red = lambda o, i, op: dve.tensor_reduce(o, i, AX_X, op)
            small_t = lambda z: z[:, 0:nt]
            big_t = lambda z: z[:, 0:nt, :]
            bank = take(dve, l, "routerT")
            ins = dve.tensor_copy(big_t(logit), bank[:, 0:nt * (NE + NG)].rearrange("p (t n) -> p t n", t=nt))
            done(ins, "D", l, "routerT")
            got(dve, "D", l, "routerT")
            for t in range(nt):
                bank = take(dve, l, "htok", t, 1)
                ins = dve.tensor_copy(htok[:, t, HALF:D], bank[:, :])
                done(ins, "D", l, "htok", t, 1)
            lg, le = big_t(logit)[:, :, NE:], big_t(logit)[:, :, 0:NE]
            gm, cm, dv, e2, den, pg, v1, v2 = [small_t(z) for z in rr]
            d4, e4, c4, o4 = [big_t(z) for z in r4]
            rev4, rev32 = bc(const("rev4"), 1, nt), bc(const("rev32"), 1, nt)
            link(red(gm, lg, ALU.max))
            ins = tt(d4, lg, bc(gm, 2, NG), ALU.subtract)
            ins.then_inc(s_ddh, 1)
            dve.wait_ge(s_ddh, 2 * l + 1)
            link(stt(c4, d4, 0.0, rev4, ALU.is_ge, ALU.mult))
            link(red(cm, c4, ALU.max))
            link(tt(o4, c4, bc(cm, 2, NG), ALU.is_equal))
            link(ts(o4, o4, 1.0, BIG, ALU.subtract, ALU.mult))
            lm, t1, t2, oh1, oh2, M = [big_t(z) for z in l32]
            link(tt(lm.rearrange("p t (g e) -> p t g e", g=NG), le.rearrange("p t (g e) -> p t g e", g=NG),
                    bc(o4, 3, EPG), ALU.add))
            for top, (v, oh) in enumerate(((v1, oh1), (v2, oh2))):
                link(red(v, lm, ALU.max))
                link(tt(t1, lm, bc(v, 2, NE), ALU.subtract))
                link(stt(t2, t1, 0.0, rev32, ALU.is_ge, ALU.mult))
                link(red(cm, t2, ALU.max))
                link(tt(oh, t2, bc(cm, 2, NE), ALU.is_equal))
                if top == 0:
                    link(stt(lm, oh, -4.0 * BIG, lm, ALU.mult, ALU.add))
            tt(M, oh1, oh2, ALU.add).then_inc(s_M, 1)
            ins = tt(dv, v2, v1, ALU.subtract)
            ins.then_inc(s_ddh, 1)
            hi = const(f"hi{l}").rearrange("p (j t) -> p j t", j=2)
            for j, oh in enumerate((oh1, oh2)):
                ts(rhs[j][:, 0:nt, 0:NE], oh, const("tok1"), None, ALU.mult)
                tt(rhs[j][:, 0:nt, NE:], oh, bc(hi[:, j, :], 2, NE), ALU.mult)
            bank = take(dve, l, "pos")
            before = bank[:, 0:nt * NE].rearrange("p (t e) -> p t e", t=nt)
            link(tt(t1, before, oh1, ALU.mult))
            ins = tt(t2, before, oh2, ALU.mult)
            done(ins, "D", l, "pos")
            got(dve, "D", l, "pos")
            red(pos[:, 0, 0:nt], t1, ALU.add)
            link(red(pos[:, 1, 0:nt], t2, ALU.add))
            dve.wait_ge(s_iota, l + 1)
            for j in range(2):
                for t in range(nt):
                    ins = ts(oneh[:, j * nt + t, 0:N], iota[:, 0:N], pos[:, j, t:t + 1], None, ALU.is_equal)
            ins.then_inc(s_oneh, 1)
            bank = take(dve, l, "cnt")
            link(dve.tensor_copy(cnt[0:NE, 0:1], bank[0:NE, 0:1]))
            ins = ts(cnt[0:NE, 1:8], const("thr", NE)[:, 0:7], bank[0:NE, 0:1], None, ALU.is_lt)
            done(ins, "D", l, "cnt")
            got(dve, "D", l, "cnt")
            red(cnt[0:NE, 8:9], cnt[0:NE, 1:8], ALU.add).then_inc(s_nb, 1)
            dve.wait_ge(s_eg, 2 * l + 2)
            link(red(den, e4, ALU.add))
            link(dve.reciprocal(pg, den))
            link(ts(den, e2, 1.0, None, ALU.add))
            link(dve.reciprocal(den, den))
            link(tt(wt[:, 0, 0:nt], den, pg, ALU.mult))
            link(tt(wt[:, 1, 0:nt], e2, wt[:, 0, 0:nt], ALU.mult))
            nb = 2 * nt
            bank = take(dve, l, "slots")
            pair = bank[:, 0:nb * 2 * NE].rearrange("p (b w e) -> p b w e", b=nb, w=2)
            f0, f1, f2 = [z[:, 0:nb, :] for z in tabf]
            link(dve.tensor_copy(f0, pair[:, :, 0, :]))
            ins = tt(f0, f0, pair[:, :, 1, :], ALU.add)
            done(ins, "D", l, "slots")
            got(dve, "D", l, "slots")
            link(ts(f1, f0, 0.0, 1.0e6, ALU.is_equal, ALU.mult))
            link(stt(f0, f0, -1.0, f1, ALU.add, ALU.add))
            link(ts(f1, f0, float(N), float(-N), ALU.is_ge, ALU.mult))
            link(tt(f1, f1, f0, ALU.add))
            ts(gtab[:, 0:nb, 0:NE], f1, 2.0, const("half"), ALU.mult, ALU.add)
            ts(stab[:, 0:nb, 0:NE], f0, 2.0, const("half"), ALU.mult, ALU.add)
            dve.memset(gtab[:, :, NE:], 2000000)
            dve.memset(stab[:, :, NE:], 2000000)
            bank = take(dve, l, "extra")
            ins = dve.tensor_copy(xtab[0:1, :], bank[0:1, 0:2 * NE])
            done(ins, "D", l, "extra")

        GATHERS = [len(range(b, NE + AHEAD, BUFS)) for b in range(BUFS)]

        block = ctx.enter_context(nc.Block())

        @block.sync
        def _(sp):
            for l in range(DEPTH):
                for local, key in enumerate(stream(l)):
                    s, _ = chunks.where[key]
                    n = key[2]
                    if local >= 4:
                        sp.wait_ge(made, jobs.at[last_use(stream(l)[local - 4])] + 1)
                    elif l:
                        sp.wait_ge(expert_free, NE * l - (s < 3))
                    if key[1] == "mod":
                        src = wmod[l][:, :, n * 512:(n + 1) * 512]
                    elif key[1] == "win":
                        src = win[l][:, :, WIN[n][0]:WIN[n][1]]
                    else:
                        src = wout[l][:, 4 * (1 - n):4 * (1 - n) + 4, :]
                    sp.dma_start(slot_view(key), src).then_inc(slot_ready[s], 16)
                for e in range(2):
                    for c in range(3):
                        s = 3 * e + c
                        if s < 4:
                            key = [k for k in stream(l) if chunks.where[k][0] == s][-1]
                            sp.wait_ge(made, jobs.at[last_use(key)] + 1)
                        else:
                            sp.wait_ge(made, jobs.at[(l, "o", LAYER_T[l] - 1)] + 1)
                        src = ewout[NE * l + e] if c == 2 else ewin[NE * l + e, c]
                        sp.dma_start(slot[s], src).then_inc(slot_ready[s], 16)
                with sp.Fori(1, NE // 2) as pair:
                    e0 = pair * 2
                    for par in range(2):
                        sp.wait_ge(expert_free, e0 + (NE * l + par - 1))
                        for c in range(3):
                            if c == 2:
                                src = ewout[bass.ds(e0 + (NE * l + par), 1), :, :].rearrange("o p n -> (o p) n")
                            else:
                                src = ewin[bass.ds(e0 + (NE * l + par), 1), c, :, :].rearrange("o p n -> (o p) n")
                            sp.dma_start(slot[3 * par + c], src).then_inc(slot_ready[3 * par + c], 16)
            for t in range(XT_TILES):
                sp.wait_ge(s_fin, t + 1)
                sp.dma_start(out[0, t * P:(t + 1) * P, :], X[:, t, :]).then_inc(s_out, 16)
            sp.wait_ge(s_out, 16 * XT_TILES)

        @block.gpsimd
        def _(pool):
            steps = [0]

            def link(ins):
                steps[0] += 1
                ins.then_inc(s_pool, 1)
                pool.wait_ge(s_pool, steps[0])

            pool.memset(csil[:, :, :], 0.0).then_inc(s_setup, 1)
            pool.memset(poolw[:, :, :], 0.0).then_inc(s_setup, 1)
            pool.memset(wgate[:, :], 0.0).then_inc(s_setup, 1)
            pool.memset(zT[:, :], 1.0).then_inc(s_setup, 1)
            for b in range(BUFS):
                pool.dma_start(spare[:, b:b + 1], t_in["c"][0, P * b:P * (b + 1)].rearrange("(p o) -> p o", o=1)) \
                    .then_inc(m_scat[b], 16)
            pool.memset(rstd, 1.0).then_inc(s_setup, 1)
            for l in range(DEPTH):
                nt = LAYER_T[l]
                vs = 2 if l < DEPTH - 1 else 1
                if l:
                    pool.wait_ge(s_comb, sum(LAYER_T[:l]))
                for v in range(vs):
                    src = t_in["b_mod"][l:l + 1, 2 * D:3 * D].broadcast_to([P, D])
                    pool.dma_start(gates[:, v, :], src).then_inc(s_gb, 16)
                pool.memset(pin[:, :, :], 0.0).then_inc(s_setup, 1)
                pool.memset(S0, 0.0).then_inc(s_setup, 1)
                n = POOL_N if nt == TILES else POOL_X
                for m in range(2):
                    got(pool, "A", l, "pool", m)
                    a, b, src = pA, pB, pin[:, m, :]
                    inv = const("inv").rearrange("p (m n) -> p m n", m=2)[:, m, :]
                    link(pool.tensor_tensor(a[:, 1:n], src[:, 0:n - 1], src[:, 1:n], ALU.add))
                    link(pool.tensor_tensor(b[:, 2:n - 1], a[:, 1:n - 2], a[:, 3:n], ALU.add))
                    if m == 1:
                        link(pool.tensor_tensor(a[:, 4:n - 3], b[:, 2:n - 5], b[:, 6:n - 1], ALU.add))
                        link(pool.tensor_tensor(b[:, 8:n - 7], a[:, 4:n - 11], a[:, 12:n - 3], ALU.add))
                    for q in range(2 if nt == TILES else 1):
                        for h, s in ((0, a), (1, b)):
                            ph = slice(64 * h, 64 * h + 64)

                            def mid(z):
                                if q:
                                    return z[ph, POOL_X + PADW:POOL_X + PADW + CTX]
                                return z[ph, 0:POOL_X].rearrange("p (r w) -> p r w", r=ROWS)[:, :, PADW:PADW + GRID_W]

                            link(pool.tensor_tensor(mid(s), mid(s), mid(inv), ALU.mult))
                            link(pool.tensor_tensor(mid(src), mid(s), mid(src), ALU.subtract))
                    pool.sem_inc(s_pdiff, 1)
                pool.wait_ge(s_res, sum(LAYER_T[:l + 1]))
                for v in range(vs):
                    src = t_in["b_mod"][l:l + 1, 5 * D:6 * D].broadcast_to([P, D])
                    pool.dma_start(gates[:, v, :], src).then_inc(s_gb, 16)
                pool.wait_ge(made, jobs.at[(l, "router")] + 1)
                pool.iota(iota, pattern=[[1, 512]], base=0, channel_multiplier=0,
                          allow_small_or_imprecise_dtypes=True).then_inc(s_iota, 1)
                got(pool, "D", l, "extra")
                pool.memset(xg[:, :, :], 0.0).then_inc(s_pool, 1)
                pool.memset(xg_x, 0.0).then_inc(s_pool, 1)
                steps[0] += 2
                pool.wait_ge(s_pool, steps[0])
                pool.wait_ge(s_hd, 16 * sum(LAYER_T[:l + 1]))
                rows_h = hd[0:2 * nt * P, :]
                rows_y = yd[0:4 * nt * P, :]
                m0 = (NE + 1) * l

                def gather(buf, e, value):
                    pool.tensor_copy(gidx[:, buf:buf + 1], gtab[:, 0, bass.ds(e, 1)]).then_inc(m_gi, 1)
                    pool.wait_ge(m_gi, value)
                    pool.sem_inc(s_mark, 1)
                    pool.indirect_dma_start(
                        out=xg[:, buf, :], out_offset=None, in_=rows_h,
                        in_offset=bass.IndirectOffsetOnAxis(ap=gidx[:, buf:buf + 1], axis=0),
                        bounds_check=2 * nt * P - 1, oob_is_err=False).then_inc(m_gath[buf], 16)

                for e in range(AHEAD):
                    gather(e, e, (NE + AHEAD) * l + e + 1)
                with pool.Fori(0, NE // BUFS) as turn:
                    e0 = turn * BUFS
                    for i in range(BUFS):
                        pool.wait_ge(m_t1, e0 + (m0 + i + 1))
                        gather((i + AHEAD) % BUFS, e0 + (i + AHEAD), e0 + ((NE + AHEAD) * l + AHEAD + i + 1))
                        pool.wait_ge(m_y, e0 + (m0 + i + 2))
                        pool.tensor_copy(sidx[:, i:i + 1], stab[:, 0, bass.ds(e0 + i, 1)]).then_inc(m_si, 1)
                        pool.wait_ge(m_si, e0 + (NE * l + i + 1))
                        pool.sem_inc(s_mark, 1)
                        pool.indirect_dma_start(
                            out=rows_y, out_offset=bass.IndirectOffsetOnAxis(ap=sidx[:, i:i + 1], axis=0),
                            in_=ye[:, i, :], in_offset=None,
                            bounds_check=4 * nt * P - 1, oob_is_err=False).then_inc(m_scat[i], 16)
                        n_x = pool.value_load(xtab[0:1, bass.ds(e0 + (NE + i), 1)], min_val=0, max_val=7)
                        k0 = pool.value_load(xtab[0:1, bass.ds(e0 + i, 1)], min_val=0, max_val=16)
                        with pool.If(n_x > 0):
                            with pool.Fori(0, n_x) as b:
                                k = k0 + b
                                row_g = gtab[:, :, :].rearrange("p b e -> p (b e)")
                                row_s = stab[:, :, :].rearrange("p b e -> p (b e)")
                                at = (b + 1) * (NE + AHEAD) + e0 + i
                                pool.tensor_copy(gidx_x[:, :], row_g[:, bass.ds(at, 1)]).then_inc(x_idx[l], 1)
                                pool.tensor_copy(sidx_x[:, :], row_s[:, bass.ds(at, 1)]).then_inc(x_idx[l], 1)
                                pool.wait_ge(x_idx[l], k * 2 + 2)
                                pool.sem_inc(s_mark, 1)
                                pool.indirect_dma_start(
                                    out=xg_x, out_offset=None, in_=rows_h,
                                    in_offset=bass.IndirectOffsetOnAxis(ap=gidx_x[:, :], axis=0),
                                    bounds_check=2 * nt * P - 1, oob_is_err=False).then_inc(x_gath[l], 16)
                                pool.wait_ge(x_y[l], k + 1)
                                pool.sem_inc(s_mark, 1)
                                pool.indirect_dma_start(
                                    out=rows_y, out_offset=bass.IndirectOffsetOnAxis(ap=sidx_x[:, :], axis=0),
                                    in_=ye_x, in_offset=None,
                                    bounds_check=4 * nt * P - 1, oob_is_err=False).then_inc(x_scat[l], 16)
                                pool.wait_ge(x_scat[l], k * 16 + 16)
                                pool.sem_inc(s_mark, 1)
                for i in range(BUFS):
                    pool.wait_ge(m_scat[i], 16 * ((NE // BUFS) * (l + 1) + 1))
                pool.sem_inc(s_zx, 1)


        @block.scalar
        def _(act):
            steps = [0]

            def link(ins):
                steps[0] += 1
                ins.then_inc(s_act, 1)
                act.wait_ge(s_act, steps[0])

            def copy(o, i, func=ACT.Copy, **kw):
                return act.activation(o, i, func, **kw)

            def load_params(l):
                n = 0

                def ld(o, i):
                    nonlocal n
                    act.dma_start(o, i).then_inc(s_par, 16)
                    n += 1

                b = t_in["b_mod"][l].rearrange("(i p k) -> p i k", p=P, k=KT)
                ld(bmod[:, :, :], b)
                ld(gnorm[:, 0, :], t_in["g_norm1"][l].rearrange("(p k) -> p k", k=KT))
                ld(gnorm[:, 1, :], t_in["g_norm2"][l].rearrange("(p k) -> p k", k=KT))
                row = lambda name: t_in[name][l:l + 1, :]
                ld(vecs[0:CONF_K, :], t_in["conf_w_dw"][l])
                ld(vecs[V_CB:V_CB + 1, :], row("conf_b_dw"))
                ld(vecs[V_LG:V_LG + 1, :], row("conf_ln_g"))
                ld(vecs[V_LB:V_LB + 1, :], row("conf_ln_b"))
                ld(vecs[V_SC:V_SC + SC_K, :], t_in["sc_w_dw"][l])
                ld(vecs[V_PS:V_PS + 1, :], row("pool_scale"))
                ld(wgate[0:RANK, 0:QK_W], t_in["gla_w_gate_f"][l])
                ld(wgate[RANK:2 * RANK, QK_W:2 * QK_W], t_in["gla_w_gate_b"][l])
                ld(wgate[2 * RANK:2 * RANK + 1, 0:QK_W], row("gla_b_gate_f"))
                ld(wgate[2 * RANK:2 * RANK + 1, QK_W:2 * QK_W], row("gla_b_gate_b"))
                ld(gout[:, :], row("gla_g_out").broadcast_to([P, GROUP_W]))
                for g in range(4):
                    h = 64 * (g % 2)
                    ld(poolw[h:h + 64, g // 2, h:h + 64], t_in["pool_w"][l, g])
                ld(wre[:, :, :], t_in["router_w_expert"][l].rearrange("(p k) n -> p k n", k=KT))
                ld(wrg[:, :, :], t_in["router_w_group"][l].rearrange("(p k) n -> p k n", k=KT))
                ld(rbias[0:NE, :], t_in["router_b_expert"][l:l + 1, :].rearrange("o n -> n o"))
                ld(rbias[NE:NE + NG, :], t_in["router_b_group"][l:l + 1, :].rearrange("o n -> n o"))
                assert n == N_PAR, n

            act.dma_start(craw[:, 0, :], t_in["c"][0].rearrange("(p k) -> p k", k=KT)).then_inc(s_in, 16)
            act.dma_start(craw[:, 1, :], t_in["c_ctx"].rearrange("(p k) -> p k", k=KT)).then_inc(s_in, 16)
            act.dma_start(cst[:, :], t_in["consts"]).then_inc(s_in, 16)
            act.dma_start(X[:, 0:XT_TILES, :], t_in["x"][0].rearrange("(t p) d -> p t d", p=P)).then_inc(s_in, 16)
            act.dma_start(X[:, XT_TILES:, :], t_in["ctx"][0].rearrange("(t p) d -> p t d", p=P)).then_inc(s_in, 16)
            act.wait_ge(s_setup, 5)
            load_params(0)
            act.wait_ge(s_in, 80)
            for v in range(2):
                act.activation(csil[:, :, v], craw[:, v, :], ACT.Silu).then_inc(s_csil, 1)

            def root_of_squares(l, n, tiles):
                for t in range(tiles):
                    if n == 1:
                        act.wait_ge(s_res, sum(LAYER_T[:l]) + t + 1)
                    elif l and t < LAYER_T[l - 1]:
                        act.wait_ge(s_comb, sum(LAYER_T[:l - 1]) + t + 1)
                    ins = act.activation(xn[:, t, :], X[:, t, :], ACT.Square, accum_out=ss[:, t:t + 1])
                link(ins)
                copy(rstd[:, 0:tiles], ss[:, 0:tiles], ACT.Sqrt, bias=const("eps"), scale=1.0 / D).then_inc(s_ss, 1)

            def norm(l, n, tiles):
                root_of_squares(l, n, tiles)
                act.wait_ge(s_rstd, 2 * l + n + 1)
                for t in range(tiles):
                    act.activation(xn[:, t, :], X[:, t, :], ACT.Copy, scale=rstd[:, t:t + 1]).then_inc(s_xn, 1)

            def mod_rows(l, i, h):
                bank = take(act, l, "mod", 2 * i + h)
                done(copy(msb[:, h, :], bank[:, :]), "A", l, "mod", 2 * i + h)

            def modulate(l, n, tiles):
                for k in range(0, KT, 2):
                    bank = take(act, l, "norm", n, k)
                    for v in range(2 if tiles == TILES else 1):
                        ins = act.activation(aT[:, k, 256 * v:256 * v + 256], bank[:, 256 * v:256 * v + 256],
                                             ACT.Identity, bias=modv[:, n, 0, v, k:k + 1],
                                             scale=modv[:, n, 1, v, k:k + 1])
                    done(ins, "A", l, "norm", n, k)

            for l in range(DEPTH):
                nt = LAYER_T[l]
                N = nt * P
                vs = 2 if l < DEPTH - 1 else 1
                n_y = sum(LAYER_T[:l])
                norm(l, 0, TILES)
                for i in (0, 1):
                    mod_rows(l, i, 0)
                    mod_rows(l, i, 1)
                act.wait_ge(s_modv, 2 * l + 1)
                modulate(l, 0, TILES)
                for m in range(2):
                    bank = take(act, l, "cgate", m)
                    done(copy(sg[:, m, 0:N], bank[:, 0:N], ACT.Sigmoid), "A", l, "cgate", m)
                for m in range(2):
                    bank = take(act, l, "scb", m)
                    done(copy(scb[:, m, 0:N], bank[:, 0:N]), "A", l, "scb", m)
                for m in range(2):
                    bank = take(act, l, "scc", m)
                    done(copy(scc[:, m, 0:N], bank[:, 0:N]), "A", l, "scc", m)
                act.wait_ge(s_setup, 5 + 2 * (l + 1))
                for m in range(2):
                    bank = take(act, l, "pool", m)
                    ins = copy(pin[:, m, 0:POOL_X].rearrange("p (r w) -> p r w", r=ROWS)[:, :, PADW:PADW + GRID_W],
                               bank[:, 0:SEQ].rearrange("p (r w) -> p r w", r=ROWS))
                    if nt == TILES:
                        ins = copy(pin[:, m, POOL_X + PADW:POOL_X + PADW + CTX], bank[:, SEQ:SEQ + CTX])
                    done(ins, "A", l, "pool", m)
                for t in range(TILES):
                    bank = take(act, l, "qkv", t)
                    a = 0 if t < nt else QK_W
                    done(copy(qkvg[:, t, a:512], bank[:, a:512]), "A", l, "qkv", t)
                bank = take(act, l, "z")
                done(copy(zT[0:2 * RANK, :], bank[0:2 * RANK, :]), "A", l, "z")
                for i in range(2):
                    bank = take(act, l, "zw", i)
                    o = lab[:, :, 2 * i:2 * i + 2, :].rearrange("p d t c -> p t d c")
                    ins = copy(o, bank[:, :].rearrange("p (t d c) -> p t d c", t=2, d=2), ACT.Abs)
                    done(ins, "A", l, "zw", i)
                got(act, "A", l, "zw", 1)
                flat = lab.rearrange("p d t c -> p (d t c)")
                link(copy(flat, flat, ACT.Exp, scale=-1.0))
                copy(flat, flat, ACT.Ln, bias=1.0).then_inc(s_lab, 1)
                for t in range(nt):
                    bank = take(act, l, "g", t)
                    done(copy(qkvg[:, t, 512:768], bank[:, 0:256], ACT.Silu), "A", l, "g", t)
                for i in (3, 4, 2):
                    mod_rows(l, i, 0)
                    mod_rows(l, i, 1)
                got(act, "D", l, "mean")
                copy(sg[:, :, 0:N], glu[:, :, 0:N], ACT.Square).then_inc(s_sq, 1)
                bank = take(act, l, "var")
                done(copy(u[:, 0, 0:N], bank[:, 0:N], ACT.Sqrt, bias=const("eps"), scale=1.0 / GROUP_W), "A", l, "var")
                for i, outs in enumerate((((0, 1.0), (1, -1.0)), ((2, 1.0),), ((3, 1.0), (4, -1.0)), ((5, 1.0),))):
                    bank = take(act, l, "cum", i)
                    for j, s in outs:
                        ins = copy(ex[:, j, :, :].rearrange("p t c -> p (t c)"), bank[:, :], ACT.Exp,
                                   scale=s / GATE_NORM)
                    done(ins, "A", l, "cum", i)
                bank = take(act, l, "dec")
                ins = copy(dec, bank[:, 0:2 * NCH].rearrange("p (i c) -> p i c", i=2), ACT.Exp, scale=1 / GATE_NORM)
                done(ins, "A", l, "dec")
                act.wait_ge(s_un, l + 1)
                for m in range(2):
                    copy(aT[:, 2 + m, 0:N], glu[:, m, 0:N], ACT.Silu, bias=chv[:, m, V_LB:V_LB + 1],
                         scale=chv[:, m, V_LG:V_LG + 1]).then_inc(s_yc, 1)
                for d in range(2):
                    bank = take(act, l, "tq", d)
                    done(copy(qdT[:, d, :], bank[:, :]), "A", l, "tq", d)
                    if d == 0:
                        act.wait_ge(s_yc, 2 * (l + 1))
                    bank = take(act, l, "tk", d)
                    done(copy(kiT[:, d, :], bank[:, :]), "A", l, "tk", d)

                def rows_T(t):
                    bank = take(act, l, "ty", t)
                    ins = copy(aT[:, 0:2, t * P:(t + 1) * P], bank[:, 0:256].rearrange("p (m n) -> p m n", m=2))
                    done(ins, "A", l, "ty", t)

                for t in range(nt):
                    bank = take(act, l, "o", t)
                    sq = ex[:, t % 2, 0:2, :].rearrange("p t c -> p (t c)")
                    if t >= 2:
                        act.wait_ge(s_y, sum(LAYER_T[:l]) + t - 1)
                    done(copy(sq, bank[:, 0:256], ACT.Square), "A", l, "o", t)
                    act.wait_ge(s_so, n_y + t + 1)
                    so = sso[:, HEADS * t:HEADS * (t + 1)]
                    copy(so, so, ACT.Sqrt, bias=const("eps"), scale=1.0 / DV).then_inc(s_ro, 1)
                    if t:
                        rows_T(t - 1)
                rows_T(nt - 1)
                for h in range(2):
                    mod_rows(l, 5, h)
                norm(l, 1, nt)
                act.wait_ge(s_modv, 2 * l + 2)
                modulate(l, 1, nt)
                bank = take(act, l, "router")
                done(copy(lgT[0:NE + NG, 0:N], bank[0:NE + NG, 0:N], ACT.Identity, bias=rbias[0:NE + NG, :]),
                     "A", l, "router")
                for t in range(nt):
                    bank = take(act, l, "htok", t, 0)
                    done(copy(htok[:, t, 0:HALF], bank[:, :]), "A", l, "htok", t, 0)
                act.wait_ge(s_ddh, 2 * l + 1)
                copy(r4[1][:, 0:nt, :], r4[0][:, 0:nt, :], ACT.Exp).then_inc(s_eg, 1)
                for t in range(nt):
                    got(act, "A", l, "htok", t, 0)
                    got(act, "D", l, "htok", t, 1)
                    dst = hd[2 * P * t:2 * P * (t + 1), :].rearrange("(p h) n -> p (h n)", h=2)
                    act.dma_start(dst, htok[:, t, :]).then_inc(s_hd, 16)
                act.wait_ge(s_ddh, 2 * l + 2)
                copy(rr[3][:, 0:nt], rr[2][:, 0:nt], ACT.Exp).then_inc(s_eg, 1)
                got(act, "D", l, "extra")
                if l + 1 < DEPTH:
                    load_params(l + 1)

                def hidden(bank, r, made_sem, value, up):
                    act.wait_ge(made_sem, value)
                    copy(r, bank[:, :]).then_inc(up, 1)

                def silu(bank, s, made_sem, value, up):
                    act.wait_ge(made_sem, value)
                    copy(s, bank[:, :].rearrange("p (k n) -> p k n", k=4)[:, :, 0:BLK], ACT.Silu).then_inc(up, 1)

                with act.Fori(0, NE // BUFS) as turn:
                    e0 = turn * BUFS
                    for i in range(BUFS):
                        par = i % 2
                        n = NE * l + i + 1
                        hidden(PS[1], raw, m_g1, e0 + n, m_raw)
                        silu(PS[2], sil, m_t2, e0 + n, m_sil)
                        n_x = act.value_load(xtab[0:1, bass.ds(e0 + (NE + i), 1)], min_val=0, max_val=7)
                        k0 = act.value_load(xtab[0:1, bass.ds(e0 + i, 1)], min_val=0, max_val=16)
                        with act.If(n_x > 0):
                            with act.Fori(0, n_x) as b:
                                k = k0 + b
                                hidden(PS[5], raw_x, x_g1[l], k + 1, x_raw[l])
                                silu(PS[6], sil_x, x_t2[l], k + 1, x_sil[l])
                act.wait_ge(s_zx, l + 1)
                for t in range(nt):
                    if t >= 2:
                        act.wait_ge(s_comb, sum(LAYER_T[:l]) + t - 1)
                    for j in range(2):
                        a = 2 * P * (j * nt + t)
                        src = yd[a:a + 2 * P, :].rearrange("(p h) n -> p (h n)", h=2)
                        act.dma_start(yin[:, t % 2, j, :], src).then_inc(s_yin[t % 2], 16)
            act.dma_start(gfin, t_in["g_final"].rearrange("(o d) -> o d", o=1).broadcast_to([P, D])).then_inc(s_gf, 16)
            root_of_squares(DEPTH, 0, XT_TILES)

        @block.tensor
        def _(pe):
            mm = pe.matmul
            tr = pe.transpose
            freed = {"A": 0, "D": 0}

            def open_(l, *key):
                i = jobs.at[(l,) + key]
                assert i == jobs.next, (key, jobs.keys[jobs.next])
                jobs.next += 1
                if i >= 8:
                    for c in jobs.readers[i - 8]:
                        if jobs.upto[i - 8][c] > freed[c]:
                            freed[c] = jobs.upto[i - 8][c]
                            pe.wait_ge(read_a if c == "A" else read_d, freed[c])
                return PS[i % 8]

            def chunk(l, *key):
                s, v = chunks.where[(l,) + key]
                pe.wait_ge(slot_ready[s], v)
                return slot_view((l,) + key)

            pe.wait_ge(s_in, 80)
            pe.wait_ge(s_csil, 2)
            def mod_product(l, n):
                w = chunk(l, "mod", n)
                bank = open_(l, "mod", n)
                for k in range(KT):
                    g = 32 * (k % 4)
                    ins = mm(bank[g:g + 32, :], csil[:, k, :], w[:, k, :], start=k < 4, stop=k >= 4)
                ins.then_inc(made, 1)

            def mod(l, i, gate):
                vs = 2 if l < DEPTH - 1 else 1
                if gate:
                    for h in range(2):
                        mod_product(l, 2 * i + h)
                        got(pe, "A", l, "mod", 2 * i + h)
                        for v in range(vs):
                            bank = open_(l, "gate", i, h, v)
                            mm(bank[:, :], const("sel_c" if v else "sel_x"), msb[:, h, :], start=True,
                               stop=True).then_inc(made, 1)
                    return
                mod_product(l, 2 * i)
                mod_product(l, 2 * i + 1)
                got(pe, "A", l, "mod", 2 * i + 1)
                bank = open_(l, "modT", i)
                for h in range(2):
                    rows = msb[:, h, :].rearrange("p (q k) -> p k q", k=KT)
                    for k in range(KT):
                        ins = mm(bank[64 * h:64 * h + 64, 2 * k:2 * k + 2], rows[:, k, :], const("sel"),
                                 start=True, stop=True)
                ins.then_inc(made, 1)

            def norm_T(l, n, tiles):
                pe.wait_ge(s_xn, sum(TILES + LAYER_T[i] for i in range(l)) + TILES * n + tiles)
                for k in range(KT):
                    bank = open_(l, "norm", n, k)
                    for t in range(tiles):
                        v = xn[:, t, :].rearrange("p (q k) -> p k q", k=KT)[:, k, :]
                        ins = tr(bank[:, t * P:(t + 1) * P], v, ident)
                    ins.then_inc(made, 1)

            for l in range(DEPTH):
                nt = LAYER_T[l]
                N = nt * P
                pe.wait_ge(s_par, 16 * N_PAR * (l + 1))
                bank = open_(l, "vec")
                for m in range(2):
                    ins = tr(bank[:, VEC_ROWS * m:VEC_ROWS * (m + 1)], vecs[0:VEC_ROWS, m * P:(m + 1) * P],
                             ident[0:VEC_ROWS, 0:VEC_ROWS])
                ins.then_inc(made, 1)
                mod(l, 0, False)
                mod(l, 1, False)
                norm_T(l, 0, TILES)
                got(pe, "A", l, "norm", 0, KT - 2)
                got(pe, "D", l, "norm", 0, KT - 1)

                def channels(w, m, *key):
                    bank = open_(l, *key)
                    for k in range(KT):
                        ins = mm(bank[:, 0:N], w[:, k, m * P:(m + 1) * P], aT[:, k, 0:N], start=k == 0,
                                 stop=k == KT - 1)
                    return ins.then_inc(made, 1)

                w = chunk(l, "win", 0)
                for m in range(2):
                    channels(w, 2 + m, "cgate", m)
                    ins = channels(w, m, "ca", m)
                w = chunk(l, "win", 1)
                for name, a in (("scb", 0), ("scc", 2)):
                    for m in range(2):
                        ins = channels(w, a + m, name, m)
                w = chunk(l, "win", 2)
                for name, a in (("scx", 0), ("pool", 2)):
                    for m in range(2):
                        ins = channels(w, a + m, name, m)
                w = chunk(l, "win", 3)
                for t in range(TILES):
                    bank = open_(l, "qkv", t)
                    a = 0 if t < nt else QK_W
                    for k in range(KT):
                        ins = mm(bank[:, a:512], aT[:, k, t * P:(t + 1) * P], w[:, k, a:512], start=k == 0,
                                 stop=k == KT - 1)
                    ins.then_inc(made, 1)
                w = chunk(l, "win", 4)
                bank = open_(l, "z")
                for k in range(KT):
                    ins = mm(bank[0:2 * RANK, :], w[:, k, 256:288], aT[:, k, :], start=k == 0, stop=k == KT - 1)
                ins.then_inc(made, 1)
                got(pe, "A", l, "z")
                for i in range(2):
                    bank = open_(l, "zw", i)
                    for t in range(2):
                        a = (2 * i + t) * P
                        ins = mm(bank[:, 256 * t:256 * t + 256], zT[0:2 * RANK + 1, a:a + P],
                                 wgate[0:2 * RANK + 1, :], start=True, stop=True)
                    ins.then_inc(made, 1)
                for t in range(nt):
                    bank = open_(l, "g", t)
                    for k in range(KT):
                        ins = mm(bank[:, 0:256], aT[:, k, t * P:(t + 1) * P], w[:, k, 0:256], start=k == 0,
                                 stop=k == KT - 1)
                    ins.then_inc(made, 1)
                mod(l, 3, False)
                mod(l, 4, False)
                mod(l, 2, True)
                pe.wait_ge(s_u, l + 1)
                bank = open_(l, "mean")
                for m in range(2):
                    ins = mm(bank[:, 0:N], ones, u[:, m, 0:N], start=m == 0, stop=m == 1)
                ins.then_inc(made, 1)
                pe.wait_ge(s_sq, l + 1)
                bank = open_(l, "var")
                for m in range(2):
                    ins = mm(bank[:, 0:N], ones, sg[:, m, 0:N], start=m == 0, stop=m == 1)
                ins.then_inc(made, 1)
                got(pe, "D", l, "zw", 1)
                for i, name in enumerate(("cum_f", "after", "cum_b", "prev")):
                    bank = open_(l, "cum", i)
                    mm(bank[:, :], const(name), la[:, i // 2, :, :].rearrange("p t c -> p (t c)"), start=True,
                       stop=True).then_inc(made, 1)
                bank = open_(l, "dec")
                for d in range(2):
                    for t in range(TILES):
                        a = 2 * (TILES * d + t)
                        ins = mm(bank[:, a:a + 2], la[:, d, t, :], const("chunks"), start=True, stop=True)
                ins.then_inc(made, 1)
                pe.wait_ge(s_pdiff, 2 * (l + 1))
                for m in range(2):
                    bank = open_(l, "pm", m)
                    rows = pin[:, m, 0:POOL_X].rearrange("p (r w) -> p r w", r=ROWS)[:, :, PADW:PADW + GRID_W]
                    ins = mm(bank[:, 0:SEQ], poolw[:, m, :], rows, start=True, stop=True)
                    if nt == TILES:
                        ins = mm(bank[:, SEQ:SEQ + CTX], poolw[:, m, :],
                                 pin[:, m, POOL_X + PADW:POOL_X + PADW + CTX], start=True, stop=True)
                    ins.then_inc(made, 1)
                for d in range(2):
                    pe.wait_ge(s_qd, 2 * l + d + 1)
                    for name, j in (("tq", 0), ("tk", 1)):
                        bank = open_(l, name, d)
                        for t in range(TILES):
                            ins = tr(bank[:, t * P:(t + 1) * P], ex[:, 3 * d + j, t, :], ident)
                        ins.then_inc(made, 1)
                for t in (2, 3, 0, 1):
                    for par in range(2):
                        bank = open_(l, "kv", t, par)
                        ph = slice(64 * par, 64 * par + 64)
                        for d in range(2):
                            ins = mm(bank[:, 256 * d:256 * d + 256], ex[ph, 3 * d + 2, t, :],
                                     qkvg[ph, t, 256:512], start=True, stop=True)
                        ins.then_inc(made, 1)
                got(pe, "A", l, "tk", 1)
                n_y = sum(LAYER_T[:l])

                def rows_T(t):
                    pe.wait_ge(s_y, n_y + t + 1)
                    bank = open_(l, "ty", t)
                    for m in range(2):
                        ins = tr(bank[:, m * P:(m + 1) * P], qkvg[:, t, 512 + m * P:640 + m * P], ident)
                    ins.then_inc(made, 1)

                for t in range(nt):
                    for d in range(2):
                        pe.wait_ge(s_qbd, 2 * (n_y + t) + d + 1)
                        bank = open_(l, "score", t, d)
                        mm(bank[:, :], kiT[:, d, t * P:(t + 1) * P], qbd[:, d, :], start=True,
                           stop=True).then_inc(made, 1)
                    if t == 0:
                        pe.wait_ge(s_S, l + 1)
                    bank = open_(l, "o", t)
                    for d in range(2):
                        for par in range(2):
                            a = t * P + 64 * par
                            mm(bank[64 * par:64 * par + 64, 0:256], qdT[:, d, a:a + 64],
                               state_in(d, 2 * t + par), start=d == 0, stop=False, skip_group_check=True)
                    for d in range(2):
                        got(pe, "D", l, "score", t, d)
                        for h in range(HEADS):
                            ins = mm(bank[:, DV * h:DV * (h + 1)], scm[:, d, h * P:(h + 1) * P],
                                     qkvg[:, t, 256 + DV * h:256 + DV * (h + 1)], start=False,
                                     stop=d == 1, skip_group_check=True)
                    ins.then_inc(made, 1)
                    if t:
                        rows_T(t - 1)
                rows_T(nt - 1)
                wa, wb = chunk(l, "wout", 0), chunk(l, "wout", 1)
                got(pe, "D", l, "pm", 1)
                pe.wait_ge(s_yc, 2 * (l + 1))
                for t in range(nt):
                    got(pe, "A", l, "ty", t)
                    for h in range(2):
                        bank = open_(l, "out", t, h)
                        for j, k in enumerate((4, 5, 6, 7, 0, 1, 2, 3)):
                            w = wa if k >= 4 else wb
                            ins = mm(bank[:, :], aT[:, k, t * P:(t + 1) * P], w[:, k % 4, 512 * h:512 * h + 512],
                                     start=j == 0, stop=j == KT - 1)
                        ins.then_inc(made, 1)
                mod(l, 5, True)
                norm_T(l, 1, nt)
                got(pe, "A", l, "norm", 1, KT - 2)
                got(pe, "D", l, "norm", 1, KT - 1)
                bank = open_(l, "router")
                for k in range(KT):
                    ins = mm(bank[0:NE + NG, 0:N], wrt[:, k, :], aT[:, k, 0:N], start=k == 0, stop=k == KT - 1)
                ins.then_inc(made, 1)
                got(pe, "A", l, "router")
                bank = open_(l, "routerT")
                for t in range(nt):
                    ins = tr(bank[:, t * (NE + NG):(t + 1) * (NE + NG)], lgT[0:NE + NG, t * P:(t + 1) * P],
                             ident[0:NE + NG, 0:NE + NG])
                ins.then_inc(made, 1)
                for t in range(nt):
                    for h in range(2):
                        bank = open_(l, "htok", t, h)
                        for k in range(4):
                            ins = tr(bank[:, k * P:(k + 1) * P], aT[:, 4 * h + k, t * P:(t + 1) * P], ident)
                        ins.then_inc(made, 1)
                pe.wait_ge(s_M, l + 1)
                M = l32[5]
                bank = open_(l, "pos")
                for t in range(nt):
                    for s in range(t + 1):
                        ins = mm(bank[:, t * NE:(t + 1) * NE], const("before") if s == t else ones, M[:, s, :],
                                 start=s == 0, stop=s == t)
                ins.then_inc(made, 1)
                bank = open_(l, "cnt")
                for t in range(nt):
                    ins = mm(bank[0:NE, 0:1], M[:, t, :], ones[:, 0:1], start=t == 0, stop=t == nt - 1)
                ins.then_inc(made, 1)
                pe.wait_ge(s_oneh, l + 1)
                bank = open_(l, "slots")
                for b in range(2 * nt):
                    for i in range(2 * nt):
                        for w in range(2):
                            ins = mm(bank[BLK * w:BLK * (w + 1), 2 * NE * b:2 * NE * (b + 1)],
                                     oneh[:, i, BLK * b:BLK * (b + 1)], rhs[i // nt][:, i % nt, :],
                                     start=i == 0, stop=i == 2 * nt - 1)
                ins.then_inc(made, 1)
                pe.wait_ge(s_nb, l + 1)
                bank = open_(l, "extra")
                mm(bank[0:1, 0:NE], cnt[0:NE, 8:9], const("before", NE)[:, 0:NE], start=True, stop=True)
                mm(bank[0:1, NE:2 * NE], cnt[0:NE, 8:9], const("ident", NE)[:, 0:NE], start=True,
                   stop=True).then_inc(made, 1)
                for c, s in (("A", read_a), ("D", read_d)):
                    pe.wait_ge(s, jobs.upto[jobs.next - 1][c])
                    freed[c] = jobs.upto[jobs.next - 1][c]
                got(pe, "D", l, "extra")

                m0 = (NE + 1) * l
                base = [chunks.where[(l, "expert", e, c)][1] for e in range(2) for c in range(3)]

                def tokens_T(bank, x, up):
                    for k in range(4):
                        ins = tr(bank[:, k * P:(k + 1) * P], x[:, k * P:(k + 1) * P], ident)
                    ins.then_inc(up, 1)

                def hidden(bank, xT, par, up, e0=None):
                    for h in range(2):
                        if e0 is not None:
                            pe.wait_ge(slot_ready[3 * par + h], e0[0] * 8 + (base[3 * par + h] + 16 * (e0[1] // 2)))
                        w = slot[3 * par + h].rearrange("p (k n) -> p k n", k=4)
                        for k in range(4):
                            for g in range(2):
                                ins = mm(bank[64 * g:64 * g + 64, :], xT[:, k, BLK * h:BLK * (h + 1)],
                                         w[:, k, 512 * g:512 * g + 512], start=h == 0 and k == 0,
                                         stop=h == 1 and k == 3)
                    ins.then_inc(up, 1)

                def hidden_T(bank, r, up):
                    v = r.rearrange("p (q k) -> p k q", k=4)
                    for k in range(4):
                        ins = tr(bank[:, k * P:(k + 1) * P], v[:, k, :], ident)
                    ins.then_inc(up, 1)

                def back(bank, h_, par, up):
                    w = slot[3 * par + 2].rearrange("p (k n) -> p k n", k=4)
                    for k in range(4):
                        for g in range(2):
                            ins = mm(bank[64 * g:64 * g + 64, :], h_[:, k, :], w[:, k, 512 * g:512 * g + 512],
                                     start=k == 0, stop=k == 3)
                    ins.then_inc(up, 1)

                pe.wait_ge(m_gath[0], 16 * (GATHERS[0] * l + 1))
                tokens_T(PS[0], xg[:, 0, :], m_t1)
                with pe.Fori(0, NE // BUFS) as turn:
                    e0 = turn * BUFS
                    for i in range(BUFS):
                        par = i % 2
                        n = NE * l + i + 1
                        pe.wait_ge(m_xeT, e0 + (m0 + i + 1))
                        hidden(PS[1], xeT[:, par, :, :], par, m_g1, (e0, i))
                        b1 = (i + 1) % BUFS
                        pe.wait_ge(m_gath[b1], turn * 16 + (16 * (GATHERS[b1] * l + 1 + (i + 1) // BUFS)))
                        tokens_T(PS[0], xg[:, b1, :], m_t1)
                        pe.wait_ge(m_raw, e0 + n)
                        hidden_T(PS[2], raw, m_t2)
                        pe.wait_ge(m_hT, e0 + n)
                        pe.wait_ge(m_y, e0 + (m0 + i + 1))
                        pe.wait_ge(slot_ready[3 * par + 2], e0 * 8 + (base[3 * par + 2] + 16 * (i // 2)))
                        back(PS[3], hT, par, m_g2)
                        n_x = pe.value_load(xtab[0:1, bass.ds(e0 + (NE + i), 1)], min_val=0, max_val=7)
                        k0 = pe.value_load(xtab[0:1, bass.ds(e0 + i, 1)], min_val=0, max_val=16)
                        with pe.If(n_x > 0):
                            with pe.Fori(0, n_x) as b:
                                k = k0 + b
                                pe.wait_ge(x_gath[l], k * 16 + 16)
                                tokens_T(PS[4], xg_x, x_t1[l])
                                pe.wait_ge(x_xeT[l], k + 1)
                                hidden(PS[5], xeT_x, par, x_g1[l])
                                pe.wait_ge(x_raw[l], k + 1)
                                hidden_T(PS[6], raw_x, x_t2[l])
                                pe.wait_ge(x_hT[l], k + 1)
                                back(PS[7], hT_x, par, x_g2[l])
                                pe.wait_ge(x_y[l], k + 1)
                        pe.wait_ge(m_g2, e0 + n)
                        pe.sem_inc(expert_free, 1)
                pe.wait_ge(m_y, m0 + NE + 1)
                pe.wait_ge(m_xeT, m0 + NE + 1)

        @block.vector
        def _(dve):
            steps = [0]

            def step(ins):
                steps[0] += 1
                ins.then_inc(s_dve, 1)
                return steps[0]

            def link(ins):
                dve.wait_ge(s_dve, step(ins))

            tt = dve.tensor_tensor
            ts = dve.tensor_scalar
            stt = dve.scalar_tensor_tensor

            def invert_rms(n):
                dve.wait_ge(s_ss, n + 1)
                dve.reciprocal(rstd, rstd).then_inc(s_rstd, 1)

            def shift_scale(l, i):
                n, what = (0, i) if i < 2 else (1, i - 3)
                bank = take(dve, l, "modT", i)
                m = bank[:, 0:2 * KT].rearrange("p (k v) -> p v k", v=2)
                b = bc(bmod[:, i, :], 1, 2)
                if what == 0:
                    done(tt(modv[:, n, 0, :, :], m, b, ALU.add), "D", l, "modT", i)
                else:
                    ins = tt(mt, m, b, ALU.add)
                    done(ins, "D", l, "modT", i)
                    got(dve, "D", l, "modT", i)
                    stt(modv[:, n, 1, :, :], mt, 1.0, bc(gnorm[:, n, :], 1, 2), ALU.add,
                        ALU.mult).then_inc(s_modv, 1)

            def gate(l, i):
                vs = 2 if l < DEPTH - 1 else 1
                before = sum(2 * (2 if q < DEPTH - 1 else 1) for q in range(l))
                dve.wait_ge(s_gb, 16 * (before + vs * (1 if i == 2 else 2)))
                for h in range(2):
                    for v in range(vs):
                        bank = take(dve, l, "gate", i, h, v)
                        g = gates[:, v, 512 * h:512 * h + 512]
                        ins = tt(g, bank[:, :], g, ALU.add)
                        done(ins, "D", l, "gate", i, h, v)
                got(dve, "D", l, "gate", i, 1, vs - 1)

            def modulate(l, n, tiles):
                for k in range(1, KT, 2):
                    bank = take(dve, l, "norm", n, k)
                    for v in range(2 if tiles == TILES else 1):
                        c = slice(256 * v, 256 * v + 256)
                        ins = ts(aT[:, k, c], bank[:, c], modv[:, n, 1, v, k:k + 1], modv[:, n, 0, v, k:k + 1],
                                 ALU.mult, ALU.add)
                    done(ins, "D", l, "norm", n, k)

            def taps(dst, src, m, row, width, both, bias):
                c = width // 2

                def part(kind):
                    for o in [0] + [s * a for a in range(1, c + 1) for s in (-1, 1)]:
                        w = chv[:, m, row + c + o:row + c + o + 1]
                        if kind == "across":
                            if abs(o) >= GRID_W:
                                continue
                            a, b = max(0, -o), GRID_W - max(0, o)
                            v = lambda z, d: z[:, m, 0:SEQ].rearrange("p (r w) -> p r w", r=ROWS)[:, :, a + d:b + d]
                        elif kind == "down":
                            if abs(o) >= ROWS:
                                continue
                            a, b = max(0, -o) * GRID_W, (ROWS - max(0, o)) * GRID_W
                            v = lambda z, d: z[:, m, a + d * GRID_W:b + d * GRID_W]
                        else:
                            a, b = SEQ + max(0, -o), SEQ + CTX - max(0, o)
                            v = lambda z, d: z[:, m, a + d:b + d]
                        if o == 0 and bias is not None:
                            yield lambda v=v, w=w: ts(v(dst, 0), v(src, 0), w, bias, ALU.mult, ALU.add)
                        elif o == 0:
                            yield lambda v=v, w=w: ts(v(dst, 0), v(src, 0), w, None, ALU.mult)
                        else:
                            yield lambda v=v, w=w, o=o: stt(v(dst, 0), v(src, o), w, v(dst, 0), ALU.mult, ALU.add)

                return [part("down" if m else "across")] + ([part("context")] if both else [])

            def run_chains(chains):
                last = [0] * len(chains)
                live = list(range(len(chains)))
                while live:
                    for i in list(live):
                        f = next(chains[i], None)
                        if f is None:
                            live.remove(i)
                            continue
                        if last[i]:
                            dve.wait_ge(s_dve, last[i])
                        last[i] = step(f())
                dve.wait_ge(s_dve, steps[0])

            for l in range(DEPTH):
                nt = LAYER_T[l]
                N = nt * P
                vs = 2 if l < DEPTH - 1 else 1
                n_y = sum(LAYER_T[:l])
                invert_rms(2 * l)
                bank = take(dve, l, "vec")
                ins = dve.tensor_copy(chv[:, :, :], bank[:, 0:2 * VEC_ROWS].rearrange("p (m v) -> p m v", m=2))
                done(ins, "D", l, "vec")
                got(dve, "D", l, "vec")
                dve.tensor_copy(wrt[:, :, 0:NE], wre[:, :, :])
                dve.tensor_copy(wrt[:, :, NE:], wrg[:, :, :])
                shift_scale(l, 0)
                shift_scale(l, 1)
                dve.wait_ge(s_modv, 2 * l + 1)
                modulate(l, 0, TILES)
                for m in range(2):
                    bank = take(dve, l, "ca", m)
                    got(dve, "A", l, "cgate", m)
                    ins = tt(glu[:, m, 0:N], bank[:, 0:N], sg[:, m, 0:N], ALU.mult)
                    done(ins, "D", l, "ca", m)
                got(dve, "D", l, "ca", 1)
                chains = []
                for m in range(2):
                    chains += taps(u, glu, m, 0, CONF_K, nt == TILES, chv[:, m, V_CB:V_CB + 1])
                run_chains(chains)
                dve.sem_inc(s_u, 1)
                for m in range(2):
                    bank = take(dve, l, "scx", m)
                    got(dve, "A", l, "scc", m)
                    ins = tt(scp[:, m, 0:N], bank[:, 0:N], scc[:, m, 0:N], ALU.mult)
                    done(ins, "D", l, "scx", m)
                got(dve, "D", l, "scx", 1)
                chains = []
                for m in range(2):
                    chains += taps(sca, scp, m, V_SC, SC_K, nt == TILES, None)
                run_chains(chains)
                dve.wait_ge(s_lab, l + 1)
                for i in range(2):
                    bank = take(dve, l, "zw", i)
                    for d in range(2):
                        z = bank[:, :].rearrange("p (t d c) -> p d t c", t=2, d=2)[:, d, :, :]
                        ins = stt(la[:, d, 2 * i:2 * i + 2, :], z, 0.0, lab[:, d, 2 * i:2 * i + 2, :], ALU.min,
                                  ALU.subtract)
                    done(ins, "D", l, "zw", i)
                for t in range(nt):
                    got(dve, "A", l, "g", t)
                    g = qkvg[:, t, 512:768]
                    ins = tt(g, g, gout[:, :], ALU.mult)
                link(ins)
                shift_scale(l, 3)
                shift_scale(l, 4)
                gate(l, 2)
                bank = take(dve, l, "mean")
                for m in range(2):
                    ins = stt(glu[:, m, 0:N], bank[:, 0:N], -1.0 / GROUP_W, u[:, m, 0:N], ALU.mult, ALU.add)
                done(ins, "D", l, "mean")
                for m in range(2):
                    tt(aT[:, 4 + m, 0:N], sca[:, m, 0:N], scb[:, m, 0:N], ALU.mult)
                got(dve, "A", l, "var")
                r = u[:, 0, 0:N]
                link(dve.reciprocal(r, r))
                for m in range(2):
                    ins = tt(glu[:, m, 0:N], glu[:, m, 0:N], r, ALU.mult)
                ins.then_inc(s_un, 1)
                for d in range(2):
                    got(dve, "A", l, "cum", 2 * d + 1)
                    q = qkvg[:, :, 0:QK_W]
                    k = qkvg[:, :, QK_W:2 * QK_W]
                    qt = TILES if nt == TILES else nt
                    stt(ex[:, 3 * d, 0:qt, :], q[:, 0:qt, :], DK ** -0.5, ex[:, 3 * d, 0:qt, :], ALU.mult, ALU.mult)
                    tt(ex[:, 3 * d + 1, :, :], k, ex[:, 3 * d + 1, :, :], ALU.mult)
                    tt(ex[:, 3 * d + 2, :, :], k, ex[:, 3 * d + 2, :, :], ALU.mult).then_inc(s_qd, 1)
                for m in range(2):
                    bank = take(dve, l, "pm", m)
                    done(ts(aT[:, 6 + m, 0:N], bank[:, 0:N], chv[:, m, V_PS:V_PS + 1], None, ALU.mult),
                         "D", l, "pm", m)
                heads = const("heads")
                got(dve, "A", l, "dec")
                for t in (2, 3, 0, 1):
                    for par in range(2):
                        c = 2 * t + par
                        bank = take(dve, l, "kv", t, par)
                        for d in range(2):
                            ins = tt(S[:, d, c, :].rearrange("p (h v) -> p h v", h=HEADS),
                                     bank[:, 256 * d:256 * d + 256].rearrange("p (h v) -> p h v", h=HEADS),
                                     bc(heads, 2, DV), ALU.mult)
                        done(ins, "D", l, "kv", t, par)
                got(dve, "D", l, "kv", 1, 1)
                for n in range(1, NCH):
                    for d in range(2):
                        c, p = ORDER[d][n], ORDER[d][n - 1]
                        v = step(stt(S[:, d, c, :], S[:, d, p, :], dec[:, d, c:c + 1], S[:, d, c, :], ALU.mult, ALU.add))
                    dve.wait_ge(s_dve, v)
                dve.sem_inc(s_S, 1)

                def q_heads(t, d):
                    got(dve, "A", l, "tq", d)
                    tt(qbd[:, d, :].rearrange("p (h i) -> p h i", h=HEADS),
                       bc(qdT[:, d, t * P:(t + 1) * P], 1, HEADS), bc(heads, 2, P), ALU.mult).then_inc(s_qbd, 1)

                q_heads(0, 0)
                q_heads(0, 1)
                for t in range(nt):
                    for d in range(2):
                        bank = take(dve, l, "score", t, d)
                        mask = bc(const("cum_b" if d else "cum_f"), 1, HEADS)
                        ins = tt(scm[:, d, :].rearrange("p (h i) -> p h i", h=HEADS),
                                 bank[:, :].rearrange("p (h i) -> p h i", h=HEADS), mask, ALU.mult)
                        done(ins, "D", l, "score", t, d)
                        if t + 1 < nt:
                            q_heads(t + 1, d)
                    bank = take(dve, l, "o", t)
                    got(dve, "A", l, "o", t)
                    sq = ex[:, t % 2, 0:2, :].rearrange("p t c -> p (t c)").rearrange("p (h v) -> p h v", h=HEADS)
                    so = sso[:, HEADS * t:HEADS * (t + 1)]
                    dve.tensor_reduce(so, sq, AX_X, ALU.add).then_inc(s_so, 1)
                    rh = ro[:, HEADS * t:HEADS * (t + 1)]
                    dve.wait_ge(s_ro, n_y + t + 1)
                    link(dve.reciprocal(rh, so))
                    o = sq
                    ins = tt(o, bank[:, 0:256].rearrange("p (h v) -> p h v", h=HEADS), bc(rh, 2, DV), ALU.mult)
                    done(ins, "D", l, "o", t)
                    got(dve, "D", l, "o", t)
                    g = qkvg[:, t, 512:768]
                    tt(g, o.rearrange("p h v -> p (h v)"), g, ALU.mult).then_inc(s_y, 1)
                for t in range(nt):
                    for h in range(2):
                        bank = take(dve, l, "out", t, h)
                        tmp = ex[:, 2 + h, :, :].rearrange("p t c -> p (t c)")
                        c = slice(512 * h, 512 * h + 512)
                        ins = tt(tmp, bank[:, :], gates[:, t // XT_TILES, c], ALU.mult)
                        done(ins, "D", l, "out", t, h)
                        got(dve, "D", l, "out", t, h)
                        ins = tt(X[:, t, c], X[:, t, c], tmp, ALU.add)
                    ins.then_inc(s_res, 1)
                gate(l, 5)
                invert_rms(2 * l + 1)
                dve.wait_ge(s_modv, 2 * l + 2)
                modulate(l, 1, nt)
                route(dve, link, tt, ts, stt, l, nt)
                m0 = (NE + 1) * l
                dve.sem_inc(m_y, 1)

                def tokens(bank, x, ms, value, up):
                    dve.wait_ge(ms, value)
                    dve.tensor_copy(x, bank[:, :].rearrange("p (k n) -> p k n", k=4)).then_inc(up, 1)

                def act_rows(bank, s, h_, ms, value, up):
                    dve.wait_ge(ms, value)
                    tt(h_, s, bank[:, :].rearrange("p (k n) -> p k n", k=4)[:, :, BLK:2 * BLK], ALU.mult).then_inc(up, 1)

                def out_rows(bank, y, ms, value, up):
                    dve.wait_ge(ms, value)
                    dve.tensor_copy(y, bank[:, :]).then_inc(up, 1)

                tokens(PS[0], xeT[:, 0, :, :], m_t1, m0 + 1, m_xeT)
                with dve.Fori(0, NE // BUFS) as turn:
                    e0 = turn * BUFS
                    for i in range(BUFS):
                        par = i % 2
                        n = NE * l + i + 1
                        tokens(PS[0], xeT[:, 1 - par, :, :], m_t1, e0 + (m0 + i + 2), m_xeT)
                        act_rows(PS[2], sil, hT, m_sil, e0 + n, m_hT)
                        dve.wait_ge(m_scat[i], turn * 16 + (16 * ((NE // BUFS) * l + 1)))
                        out_rows(PS[3], ye[:, i, :], m_g2, e0 + n, m_y)
                        n_x = dve.value_load(xtab[0:1, bass.ds(e0 + (NE + i), 1)], min_val=0, max_val=7)
                        k0 = dve.value_load(xtab[0:1, bass.ds(e0 + i, 1)], min_val=0, max_val=16)
                        with dve.If(n_x > 0):
                            with dve.Fori(0, n_x) as b:
                                k = k0 + b
                                tokens(PS[4], xeT_x, x_t1[l], k + 1, x_xeT[l])
                                act_rows(PS[6], sil_x, hT_x, x_sil[l], k + 1, x_hT[l])
                                out_rows(PS[7], ye_x, x_g2[l], k + 1, x_y[l])
                for t in range(nt):
                    b = t % 2
                    seen = sum((LAYER_T[q] - b + 1) // 2 for q in range(l)) + t // 2 + 1
                    dve.wait_ge(s_yin[b], 32 * seen)
                    y1, y2 = yin[:, b, 0, :], yin[:, b, 1, :]
                    link(ts(y1, y1, wt[:, 0, t:t + 1], None, ALU.mult))
                    link(stt(y1, y2, wt[:, 1, t:t + 1], y1, ALU.mult, ALU.add))
                    link(tt(y1, y1, gates[:, t // XT_TILES, :], ALU.mult))
                    tt(X[:, t, :], X[:, t, :], y1, ALU.add).then_inc(s_comb, 1)
            invert_rms(2 * DEPTH)
            dve.wait_ge(s_rstd, 2 * DEPTH + 1)
            dve.wait_ge(s_gf, 16)
            for t in range(XT_TILES):
                stt(X[:, t, :], X[:, t, :], rstd[:, t:t + 1], gfin, ALU.mult, ALU.mult).then_inc(s_fin, 1)


_INS = ['x', 'c', 'ctx', 'c_ctx', 'w_mod', 'b_mod', 'g_norm1', 'g_norm2', 'w_in', 'gla_w_gate_f', 'gla_b_gate_f',
        'gla_w_gate_b', 'gla_b_gate_b', 'gla_g_out', 'conf_w_dw', 'conf_b_dw', 'conf_ln_g', 'conf_ln_b', 'sc_w_dw',
        'pool_w', 'pool_scale', 'w_out', 'router_w_group', 'router_b_group', 'router_w_expert', 'router_b_expert',
        'expert_w_in', 'expert_w_out', 'g_final']


def kernel(**inputs):
    import numpy as _np
    import concourse.bacc as _bacc
    from concourse import mybir as _mybir
    from concourse.bass_utils import run_bass_kernel_spmd as _run

    nc = _bacc.Bacc("TRN2", target_bir_lowering=False, num_devices=1)
    arrays, args = {}, {}
    for name in _INS:
        a = _np.ascontiguousarray(inputs[name])
        arrays[f"in_{name}"] = a
        args[name] = nc.dram_tensor(f"in_{name}", a.shape, _mybir.dt.from_np(a.dtype), kind="ExternalInput").ap()
    arrays["in_consts"] = constants()
    args["consts"] = nc.dram_tensor("in_consts", (P, CONST_N), F32, kind="ExternalInput").ap()
    o = nc.dram_tensor("out_0", (1, SEQ, D), F32, kind="ExternalOutput").ap()
    build(nc, args, o)
    r = _run(nc, [arrays], core_ids=[0])
    return r.results[0]["out_0"]
```

```python
import numpy as np
from contextlib import ExitStack

import concourse.bass as bass
from concourse import mybir

ALU = mybir.AluOpType
ACT = mybir.ActivationFunctionType
F32 = mybir.dt.float32
BF16 = mybir.dt.bfloat16
I32 = mybir.dt.int32
U32 = mybir.dt.uint32
AX_X = mybir.AxisListType.X

P = 128
D = 1024
KT = D // P
DEPTH = 2
SEQ = 256
CTX = 256
XT_TILES = SEQ // P
TILES = (SEQ + CTX) // P
GRID_W = 64
ROWS = SEQ // GRID_W
GROUP_W = D // 4
HEADS = 4
DV = GROUP_W // HEADS
DK = DV // 2
QK_W = HEADS * DK
RANK = 16
GATE_NORM = 16.0
CHUNK = 64
NCH = TILES * 2
CONF_K = 31
SC_K = 3
WINDOWS = (2, 4, 8, 16)
N_IN = 2 * QK_W + 2 * RANK + 8 * GROUP_W
NG = 4
EPG = 8
NE = NG * EPG
DE = D // 2
EPS = 1e-6
BIG = 1.0e30
BUFS = 4
AHEAD = BUFS - 1
BLK = 64
HALF = D // 2
VEC_ROWS = CONF_K + 3 + SC_K + 1
V_CB, V_LG, V_LB, V_SC, V_PS = CONF_K, CONF_K + 1, CONF_K + 2, CONF_K + 3, CONF_K + 3 + SC_K

C_Q, C_G, C_Z = 0, 2 * QK_W + GROUP_W, 2 * QK_W + 2 * GROUP_W
C_CONF = C_Z + 2 * RANK
C_SC = C_CONF + 2 * GROUP_W
C_XP = C_SC + 2 * GROUP_W
PADW = 8
PX = GRID_W + 2 * PADW
POOL_X = ROWS * PX
POOL_N = POOL_X + CTX + 2 * PADW


def layer_tiles(l):
    return XT_TILES if l == DEPTH - 1 else TILES


CONST_COLS = {}


def _const_layout():
    at = 0
    for name, n in (("ident", P), ("ones", P), ("before", P), ("cum_f", P), ("cum_b", P), ("after", P),
                    ("prev", P), ("sel", 2), ("heads", HEADS), ("eps", 1), ("chunks", 2),
                    ("tok1", 1), ("half", 1), ("rev4", NG), ("rev32", NE), ("thr", 8),
                    ("hi0", 2 * TILES), ("hi1", 2 * XT_TILES), ("inv", 2 * POOL_N)):
        CONST_COLS[name] = (at, n)
        at += n
    return at


CONST_N = _const_layout()


def constants():
    c = np.zeros((P, CONST_N), np.float32)

    def put(name, v):
        a, n = CONST_COLS[name]
        c[:, a:a + n] = v

    j, i = np.arange(P)[:, None], np.arange(P)[None, :]
    same = (j // CHUNK) == (i // CHUNK)
    put("ident", j == i)
    put("ones", 1.0)
    put("before", j < i)
    put("cum_f", same & (j <= i))
    put("cum_b", same & (j >= i))
    put("after", same & (j > i))
    put("prev", same & (j < i))
    put("sel", (j % 32) == np.arange(2)[None, :])
    put("heads", (j // DK) == np.arange(HEADS)[None, :])
    put("eps", EPS)
    put("chunks", (j // CHUNK) == np.arange(2)[None, :])
    put("tok1", j + 1)
    put("half", j // BLK)
    put("rev4", NG - np.arange(NG)[None, :])
    put("rev32", NE - np.arange(NE)[None, :])
    put("thr", BLK * (1 + np.arange(8))[None, :])
    for l in range(2):
        nt = layer_tiles(l)
        put(f"hi{l}", np.array([cj * nt * P + t * P for cj in range(2) for t in range(nt)])[None, :])
    inv = np.zeros((P, 2, POOL_N), np.float32)

    def counts(length, win):
        t = np.arange(length)
        return np.clip(t + win // 2, 0, length) - np.clip(t - win // 2, 0, length)

    for g, win in enumerate(WINDOWS):
        parts = slice(64 * (g % 2), 64 * (g % 2) + 64)
        for r in range(ROWS):
            inv[parts, g // 2, r * PX + PADW:r * PX + PADW + GRID_W] = 1.0 / counts(GRID_W, win)
        inv[parts, g // 2, POOL_X + PADW:POOL_X + PADW + CTX] = 1.0 / counts(CTX, win)
    put("inv", inv.reshape(P, -1))
    return c


def gla_steps(l):
    nt = layer_tiles(l)
    outs = [("out", t, h) for t in range(nt) for h in range(2)]
    late = [("mod", 8), ("mod", 9), ("modT", 4)]
    steps = [("scores", 0)]
    for t in range(nt):
        if t + 1 < nt:
            steps.append(("scores", t + 1))
        if t == 0:
            steps += [("mod", 6), ("mod", 7)]
        if t == 1 and t == nt - 1:
            steps += late
            late = []
        steps.append(("o", t))
        if t == 0:
            steps.append(("modT", 3))
        if t:
            steps += [("ty", t - 1), outs.pop(0)]
    if nt > 2:
        steps.append(outs.pop(0))
    steps.append(("ty", nt - 1))
    return steps + [outs.pop(0)] + late + outs + [("mod", 10), ("mod", 11)]


def psum_jobs(l):
    nt = layer_tiles(l)
    jobs = [(("mod", 0), "A"), (("mod", 1), "A"), (("modT", 0), "D"), (("mod", 2), "A"), (("mod", 3), "A"),
            (("modT", 1), "D"), (("vec",), "D")]
    jobs += [(("norm", 0, k), "AD"[k % 2]) for k in range(KT)]
    jobs += [(("cgate", 0), "A"), (("ca", 0), "D"), (("cgate", 1), "A"), (("ca", 1), "D")]
    jobs += [(("scb", 0), "A"), (("scb", 1), "A"), (("scc", 0), "A"), (("scc", 1), "A")]
    jobs += [(("scx", 0), "D"), (("scx", 1), "D"), (("pool", 0), "A"), (("pool", 1), "A")]
    jobs += [(("z",), "A")]
    jobs += [(("zw", 0), "AD"), (("zw", 1), "AD"), (("mean",), "D")]
    jobs += [(("g", t), "A") for t in range(nt)]
    jobs += [(("var",), "A")]
    jobs += [(("cum", i), "A") for i in range(4)] + [(("dec",), "A")]
    jobs += [(("qkv", 0), "A"), (("pm", 0), "D"), (("pm", 1), "D")]
    jobs += [(("qkv", t), "A") for t in range(1, TILES)]
    jobs += [(("mod", 4), "A"), (("mod", 5), "A")]
    jobs += [(("tq", 0), "A"), (("tk", 0), "A"), (("modT", 2), "D"), (("tq", 1), "A"), (("tk", 1), "A")]
    jobs += [(("kv", t, par), "D") for t in (2, 3, 0, 1) for par in range(2)]
    readers = {"mod": "A", "modT": "D", "o": "AD", "ty": "A", "out": "D"}
    for k in gla_steps(l):
        if k[0] == "scores":
            jobs += [(("score", k[1], 0), "D"), (("score", k[1], 1), "D")]
        else:
            jobs.append((k, readers[k[0]]))
    jobs += [(("norm", 1, k), "AD"[k % 2]) for k in range(KT)]
    jobs += [(("router",), "A"), (("routerT",), "D")]
    jobs += [(("htok", t, h), "A") for t in range(nt) for h in range(2)]
    jobs += [(("pos",), "D"), (("cnt",), "D"), (("slots",), "D"), (("extra",), "D"), (("modT", 5), "D")]
    return [((l,) + k, c) for k, c in jobs]


class PsumJobs:

    def __init__(self, jobs):
        self.keys = [k for k, _ in jobs]
        self.readers = [c for _, c in jobs]
        self.at = {k: i for i, k in enumerate(self.keys)}
        self.taken = {"A": [], "D": []}
        self.upto = []
        n = {"A": 0, "D": 0}
        for c in self.readers:
            for x in c:
                n[x] += 1
            self.upto.append(dict(n))
        self.next = 0

    def bank(self, *key):
        return self.at[key] % 8


class Ring:

    def __init__(self):
        self.count = [0] * 6
        self.where = {}

    def add(self, key, slot):
        self.count[slot] += 16
        self.where[key] = (slot, self.count[slot])


def stream(l):
    first = [(l, "mod", n) for n in range(4)] + [(l, "win", n) for n in (0, 1, 2, 4, 3)]
    return first + [(l, "mod", n) for n in range(4, 8)] + [(l, "wout", 0), (l, "wout", 1)] + \
        [(l, "mod", n) for n in range(8, 12)]


STREAM_SLOTS = [0, 1, 2, 3, 0, 1, 2, 3, 0, 1, 2, 3, 0, 1, 2, 3, 0, 3, 0]


def build(nc, t_in, out):
    ctx = ExitStack()
    with ctx:
        def sb(name, shape, dt=F32):
            return ctx.enter_context(nc.sbuf_tensor(name, shape, dt))

        def sem(name):
            return ctx.enter_context(nc.semaphore(name))

        SLOT = 4 * D
        ring = sb("ring", [P, 6 * SLOT])
        X = sb("resid", [P, TILES, D])
        gates = sb("gates", [P, 2, D])
        actT = sb("actT", [P, KT * TILES * P])
        work = sb("work", [P, 6144])
        states = sb("states", [P, 2 * NCH * 256 + 256])
        zT = sb("zT", [P, TILES * P])
        cst = sb("cst", [P, CONST_N])
        wgate = sb("wgate", [P, 256])
        gout = sb("gout", [P, GROUP_W])
        vecs = sb("vecs", [P, GROUP_W])
        chv = sb("chv", [P, 2, VEC_ROWS])
        poolw = sb("poolw", [P, 2, P])
        wre = sb("wre", [P, KT, NE])
        wrg = sb("wrg", [P, KT, NG])
        wrt = sb("wrt", [P, KT, NE + NG])
        rbias = sb("rbias", [P, 1])
        gnorm = sb("gnorm", [P, 2, KT])
        bmod = sb("bmod", [P, 6, KT])
        modv = sb("modv", [P, 2, 2, 2, KT])
        msb = sb("msb", [P, 2, 512])
        gvec = sb("gvec", [P, 2, 2, KT])
        csil = sb("csil", [P, KT, 32])
        craw = sb("craw", [P, 2, KT])
        small = sb("small", [P, 600])
        gtab = sb("gtab", [P, 8, NE + AHEAD], I32)
        stab = sb("stab", [P, 8, NE + AHEAD], I32)
        xtab = sb("xtab", [1, 2 * NE], I32)
        gidx = sb("gidx", [P, BUFS], U32)
        sidx = sb("sidx", [P, BUFS], U32)
        spare = sb("spare", [P, BUFS])
        gidx_x = sb("gidx_x", [P, 1], U32)
        sidx_x = sb("sidx_x", [P, 1], U32)

        PS = [ctx.enter_context(nc.psum_tensor(f"bank{i}", [P, 512], F32)) for i in range(8)]
        hd = nc.dram_tensor("h_rows", [2 * TILES * P, HALF], F32, kind="Internal").ap()
        gd = nc.dram_tensor("gate_rows", [2 * 2 * DEPTH, D], F32, kind="Internal").ap()
        yd = nc.dram_tensor("y_rows", [2 * 2 * TILES * P, HALF], F32, kind="Internal").ap()

        def const(name, parts=P):
            a, n = CONST_COLS[name]
            return cst[0:parts, a:a + n]

        def cut(t, a, n, dt=None):
            v = t[:, a:a + n]
            return v if dt is None else v.bitcast(dt)

        def bc(ap, axis, n):
            v = ap.unsqueeze(axis)
            shape = list(v.shape)
            shape[axis] = n
            return v.broadcast_to(shape)

        ident = const("ident")
        ones = const("ones")
        slot = [ring[:, s * SLOT:(s + 1) * SLOT] for s in range(6)]
        aT = actT[:, :].rearrange("p (k t) -> p k t", k=KT)
        xn = work[:, 0:4096].rearrange("p (t d) -> p t d", t=TILES)
        qkvg = work[:, 0:3072].rearrange("p (t c) -> p t c", t=TILES)
        ex = work[:, 3072:6144].rearrange("p (i t c) -> p i t c", i=6, t=TILES)
        conv = ring[:, 4 * SLOT:6 * SLOT]
        sg = conv[:, 0:1024].rearrange("p (m t) -> p m t", m=2)
        glu = conv[:, 1024:2048].rearrange("p (m t) -> p m t", m=2)
        u = conv[:, 2048:3072].rearrange("p (m t) -> p m t", m=2)
        scb = conv[:, 3072:4096].rearrange("p (m t) -> p m t", m=2)
        scc = conv[:, 4096:5120].rearrange("p (m t) -> p m t", m=2)
        scp = conv[:, 5120:6144].rearrange("p (m t) -> p m t", m=2)
        sca = conv[:, 6144:7168].rearrange("p (m t) -> p m t", m=2)
        la = conv[:, 7168:8192].rearrange("p (i t c) -> p i t c", i=2, t=TILES)
        lab = ex[:, 0:2, :, :]
        qdT = scc.rearrange("p m t -> p (m t)").rearrange("p (m t) -> p m t", m=2)
        kiT = sg
        scm = scp
        qbd = scb
        S = states[:, 0:2 * NCH * 256].rearrange("p (i c n) -> p i c n", i=2, c=NCH)
        S0 = states[:, 2 * NCH * 256:]
        pin = states[:, 0:2 * POOL_N].rearrange("p (m n) -> p m n", m=2)
        pA = states[:, 2 * POOL_N:3 * POOL_N]
        pB = states[:, 3 * POOL_N:4 * POOL_N]
        htok = states[:, 0:4096].rearrange("p (t d) -> p t d", t=TILES)
        oneh = work[:, 4096:6144].bitcast(BF16).rearrange("p (n s) -> p n s", s=512)
        iota = work[:, 2048:2560]
        xg = work[:, 0:2048].rearrange("p (b n) -> p b n", b=BUFS)
        xeT = work[:, 2048:3072].rearrange("p (b k n) -> p b k n", b=2, k=4)
        raw = work[:, 3072:3584]
        sil = work[:, 3584:3840].rearrange("p (k n) -> p k n", k=4)
        hT = work[:, 3840:4096].rearrange("p (k n) -> p k n", k=4)
        ye = work[:, 4096:6144].rearrange("p (b n) -> p b n", b=BUFS)
        xg_x = actT[:, 0:512]
        xeT_x = actT[:, 512:1024].rearrange("p (k n) -> p k n", k=4)
        raw_x = actT[:, 1024:1536]
        sil_x = actT[:, 1536:1792].rearrange("p (k n) -> p k n", k=4)
        hT_x = actT[:, 1792:2048].rearrange("p (k n) -> p k n", k=4)
        ye_x = actT[:, 2048:2560]
        yin = [z.rearrange("p (j d) -> p j d", j=2)
               for z in (states[:, 0:2048], states[:, 2048:4096], slot[4][:, 0:2048], slot[4][:, 2048:4096])]
        gfin = actT[:, 2560:3584]
        sqt = actT[:, 2560:3584]

        class Small:
            at = 0

            def __call__(self, n):
                self.at += n
                assert self.at <= 600
                return small[:, self.at - n:self.at]

        sm = Small()
        ss = sm(TILES)
        rstd = sm(TILES)
        sso = sm(TILES * HEADS)
        ro = sm(TILES * HEADS)
        dec = sm(2 * NCH).rearrange("p (i c) -> p i c", i=2)
        mt = sm(2 * KT).rearrange("p (v k) -> p v k", v=2)
        logit = sm(TILES * (NE + NG)).rearrange("p (t n) -> p t n", t=TILES)
        r4 = [sm(TILES * NG).rearrange("p (t n) -> p t n", t=TILES) for _ in range(4)]
        rr = [sm(TILES) for _ in range(8)]
        wt = sm(2 * TILES).rearrange("p (j t) -> p j t", j=2)
        pos = sm(2 * TILES).rearrange("p (j t) -> p j t", j=2)
        cnt = sm(9)
        l32 = [work[:, 512 + 128 * i:640 + 128 * i].rearrange("p (t n) -> p t n", t=TILES) for i in range(6)]
        rhs = [work[:, 1280 + 128 * i:1408 + 128 * i].bitcast(BF16).rearrange("p (t n) -> p t n", t=TILES)
               for i in range(2)]
        tabf = [work[:, 2560 + 256 * i:2816 + 256 * i].rearrange("p (b e) -> p b e", b=8) for i in range(3)]
        lgT = work[:, 3328:3840]
        made, read_a, read_d = sem("made"), sem("read_a"), sem("read_d")
        slot_ready = [sem(f"slot_ready{s}") for s in range(6)]
        expert_free = sem("experts_read")
        s_c = sem("conditions_loaded")
        s_cst = sem("constants_loaded")
        s_in = sem("inputs_loaded")
        s_mpar = sem("modulation_params_loaded")
        s_par = sem("params_loaded")
        s_gs = sem("gate_rows_stored")
        s_gb = sem("gates_loaded")
        s_dve, s_act, s_pool = sem("vector_step"), sem("scalar_step"), sem("pool_step")
        s_setup = sem("pool_zeroed")
        s_csil = sem("silu_c")
        s_modv = sem("modulation_ready")
        s_ss = sem("squares_summed")
        s_rstd = sem("rstd_ready")
        s_so, s_ro = sem("o_squares_summed"), sem("o_rstd")
        s_xn = sem("normed")
        s_pdiff = sem("pool_diff_ready")
        s_lab = sem("log1p_ready")
        s_u = sem("conf_u_ready")
        s_sq = sem("conf_squared")
        s_yc = sem("conf_rows_ready")
        s_un = sem("conf_normed")
        s_qd = sem("decayed_qk_ready")
        s_S = sem("states_ready")
        s_qbd = sem("q_by_heads")
        s_y = sem("gla_rows_ready")
        s_res = sem("residual_added")
        s_ddh = sem("exp_input_ready")
        s_eg = sem("group_exp_ready")
        s_hd = sem("h_rows_stored")
        s_M = sem("choices_ready")
        s_oneh = sem("positions_onehot")
        s_nb = sem("block_counts")
        s_iota = sem("iota_loaded")
        m_gi, m_si = sem("m_gather_index"), sem("m_scatter_index")
        m_gath = [sem(f"m_gathered{b}") for b in range(BUFS)]
        m_scat = [sem(f"m_scattered{b}") for b in range(BUFS)]
        m_t1, m_xeT, m_g1, m_raw = sem("m_transposed"), sem("m_tokens_ready"), sem("m_hidden"), sem("m_hidden_sb")
        m_t2, m_sil, m_hT, m_g2, m_y = sem("m_hidden_T"), sem("m_silu"), sem("m_act_ready"), sem("m_out"), sem("m_out_sb")
        x_names = ("indices", "gathered", "transposed", "tokens_ready", "hidden", "hidden_sb", "hidden_T", "silu",
                   "act_ready", "out", "out_sb", "scattered")
        x_idx, x_gath, x_t1, x_xeT, x_g1, x_raw, x_t2, x_sil, x_hT, x_g2, x_y, x_scat = [
            [sem(f"x_{n}{l}") for l in range(DEPTH)] for n in x_names]
        s_w1 = sem("first_output_weighted")
        s_yin = [sem(f"y_loaded{t}") for t in range(TILES)]
        s_mark = sem("pool_goes_on")
        s_paced = sem("stream_goes_on")
        s_comb = sem("combined")
        s_gf = sem("final_gain_loaded")
        s_fin = sem("final_rows")
        s_out = sem("stored")

        jobs = PsumJobs([j for l in range(DEPTH) for j in psum_jobs(l)])
        chunks = Ring()
        for l in range(DEPTH):
            for n, key in enumerate(stream(l)):
                chunks.add(key, STREAM_SLOTS[n])
            for e in range(NE):
                for c in range(3):
                    chunks.add((l, "expert", e, c), 3 * (e % 2) + c)
        N_PAR = 21
        LAYER_T = [layer_tiles(l) for l in range(DEPTH)]

        def take(eng, l, *key):
            i = jobs.at[(l,) + key]
            eng.wait_ge(made, i + 1)
            return PS[i % 8]

        def done(ins, who, l, *key):
            i = jobs.at[(l,) + key]
            jobs.taken[who].append(i)
            assert jobs.taken[who] == sorted(jobs.taken[who]) and jobs.upto[i][who] == len(jobs.taken[who]), key
            return ins.then_inc(read_a if who == "A" else read_d, 1)

        def got(eng, who, l, *key):
            eng.wait_ge(read_a if who == "A" else read_d, jobs.upto[jobs.at[(l,) + key]][who])

        def last_use(key):
            l, name, n = key
            if name == "mod":
                return key
            if name == "wout":
                return (l, "out", LAYER_T[l] - 1, 1)
            return ((l, "ca", 1), (l, "scc", 1), (l, "pool", 1), (l, "qkv", TILES - 1), (l, "g", LAYER_T[l] - 1))[n]

        def norm_base(l, n):
            return sum(TILES + LAYER_T[i] for i in range(l)) + TILES * n

        def yin_loads(l, t):
            return sum(LAYER_T[q] > t for q in range(l + 1))

        GATE_LOADS = {}
        for l in range(DEPTH):
            for i in (2, 5):
                GATE_LOADS[l, i] = len(GATE_LOADS) + 1

        wmod = [t_in["w_mod"][l].rearrange("(p k) n -> p k n", k=KT) for l in range(DEPTH)]
        win = [t_in["w_in"][l].rearrange("(p k) n -> p k n", k=KT) for l in range(DEPTH)]
        wout = [t_in["w_out"][l].rearrange("(k p) n -> p k n", p=P) for l in range(DEPTH)]
        WIN = [(C_CONF, C_SC), (C_SC, C_XP), (C_XP, N_IN), (C_Q, C_G), (C_G, C_CONF)]
        ewin = t_in["expert_w_in"].rearrange("l e (p h k) n -> (l e) h p (k n)", h=2, k=4)
        ewout = t_in["expert_w_out"].rearrange("l e (p k) n -> (l e) p (k n)", k=4)

        def slot_view(key):
            s, _ = chunks.where[key]
            v = slot[s]
            if key[1] == "mod":
                return v.rearrange("p (k n) -> p k n", k=KT)
            if key[1] == "win":
                a, b = WIN[key[2]]
                return v[:, 0:KT * (b - a)].rearrange("p (k n) -> p k n", k=KT)
            return v.rearrange("p (k n) -> p k n", k=4)

        ORDER = [[4, 5, 6, 7, 0, 1, 2, 3], [7, 6, 5, 4, 3, 2, 1, 0]]

        def state_in(d, c):
            n = ORDER[d].index(c)
            return S[:, d, ORDER[d][n - 1], :] if n else S0

        def route(dve, link, tt, ts, stt, shift_scale, l, nt):
            N = nt * P
            red = lambda o, i, op: dve.tensor_reduce(o, i, AX_X, op)
            small_t = lambda z: z[:, 0:nt]
            big_t = lambda z: z[:, 0:nt, :]
            bank = take(dve, l, "routerT")
            ins = dve.tensor_copy(big_t(logit), bank[:, 0:nt * (NE + NG)].rearrange("p (t n) -> p t n", t=nt))
            done(ins, "D", l, "routerT")
            got(dve, "D", l, "routerT")
            lg, le = big_t(logit)[:, :, NE:], big_t(logit)[:, :, 0:NE]
            gm, cm, dv, e2, den, pg, v1, v2 = [small_t(z) for z in rr]
            d4, e4, c4, o4 = [big_t(z) for z in r4]
            rev4, rev32 = bc(const("rev4"), 1, nt), bc(const("rev32"), 1, nt)
            link(red(gm, lg, ALU.max))
            ins = tt(d4, lg, bc(gm, 2, NG), ALU.subtract)
            ins.then_inc(s_ddh, 1)
            dve.wait_ge(s_ddh, 2 * l + 1)
            link(stt(c4, d4, 0.0, rev4, ALU.is_ge, ALU.mult))
            link(red(cm, c4, ALU.max))
            link(tt(o4, c4, bc(cm, 2, NG), ALU.is_equal))
            link(ts(o4, o4, 1.0, BIG, ALU.subtract, ALU.mult))
            lm, t1, t2, oh1, oh2, M = [big_t(z) for z in l32]
            link(tt(lm.rearrange("p t (g e) -> p t g e", g=NG), le.rearrange("p t (g e) -> p t g e", g=NG),
                    bc(o4, 3, EPG), ALU.add))
            for top, (v, oh) in enumerate(((v1, oh1), (v2, oh2))):
                link(red(v, lm, ALU.max))
                link(tt(t1, lm, bc(v, 2, NE), ALU.subtract))
                link(stt(t2, t1, 0.0, rev32, ALU.is_ge, ALU.mult))
                link(red(cm, t2, ALU.max))
                link(tt(oh, t2, bc(cm, 2, NE), ALU.is_equal))
                if top == 0:
                    link(stt(lm, oh, -4.0 * BIG, lm, ALU.mult, ALU.add))
            tt(M, oh1, oh2, ALU.add).then_inc(s_M, 1)
            ins = tt(dv, v2, v1, ALU.subtract)
            ins.then_inc(s_ddh, 1)
            hi = const(f"hi{l}").rearrange("p (j t) -> p j t", j=2)
            for j, oh in enumerate((oh1, oh2)):
                ts(rhs[j][:, 0:nt, 0:NE], oh, const("tok1"), None, ALU.mult)
                tt(rhs[j][:, 0:nt, NE:], oh, bc(hi[:, j, :], 2, NE), ALU.mult)
            bank = take(dve, l, "pos")
            before = bank[:, 0:nt * NE].rearrange("p (t e) -> p t e", t=nt)
            link(tt(t1, before, oh1, ALU.mult))
            ins = tt(t2, before, oh2, ALU.mult)
            done(ins, "D", l, "pos")
            got(dve, "D", l, "pos")
            red(pos[:, 0, 0:nt], t1, ALU.add)
            link(red(pos[:, 1, 0:nt], t2, ALU.add))
            dve.wait_ge(s_iota, l + 1)
            for j in range(2):
                for t in range(nt):
                    ts(oneh[:, j * nt + t, 0:N], iota[:, 0:N], pos[:, j, t:t + 1], None,
                       ALU.is_equal).then_inc(s_oneh, 1)
            bank = take(dve, l, "cnt")
            link(dve.tensor_copy(cnt[0:NE, 0:1], bank[0:NE, 0:1]))
            ins = ts(cnt[0:NE, 1:8], const("thr", NE)[:, 0:7], bank[0:NE, 0:1], None, ALU.is_lt)
            done(ins, "D", l, "cnt")
            got(dve, "D", l, "cnt")
            red(cnt[0:NE, 8:9], cnt[0:NE, 1:8], ALU.add).then_inc(s_nb, 1)
            dve.wait_ge(s_eg, 2 * l + 2)
            link(red(den, e4, ALU.add))
            link(dve.reciprocal(pg, den))
            link(ts(den, e2, 1.0, None, ALU.add))
            link(dve.reciprocal(den, den))
            link(tt(wt[:, 0, 0:nt], den, pg, ALU.mult))
            link(tt(wt[:, 1, 0:nt], e2, wt[:, 0, 0:nt], ALU.mult))
            nb = 2 * nt
            bank = take(dve, l, "slots")
            pair = bank[:, 0:nb * 2 * NE].rearrange("p (b w e) -> p b w e", b=nb, w=2)
            f0, f1, f2 = [z[:, 0:nb, :] for z in tabf]
            link(dve.tensor_copy(f0, pair[:, :, 0, :]))
            ins = tt(f0, f0, pair[:, :, 1, :], ALU.add)
            done(ins, "D", l, "slots")
            got(dve, "D", l, "slots")
            link(ts(f1, f0, 0.0, 1.0e6, ALU.is_equal, ALU.mult))
            link(stt(f0, f0, -1.0, f1, ALU.add, ALU.add))
            link(ts(f1, f0, float(N), float(-N), ALU.is_ge, ALU.mult))
            link(tt(f1, f1, f0, ALU.add))
            ts(gtab[:, 0:nb, 0:NE], f1, 2.0, const("half"), ALU.mult, ALU.add)
            ts(stab[:, 0:nb, 0:NE], f0, 2.0, const("half"), ALU.mult, ALU.add)
            dve.memset(gtab[:, :, NE:], 2000000)
            dve.memset(stab[:, :, NE:], 2000000)
            bank = take(dve, l, "extra")
            ins = dve.tensor_copy(xtab[0:1, :], bank[0:1, 0:2 * NE])
            done(ins, "D", l, "extra")
            shift_scale(l, 5)

        GATHERS = [len(range(b, NE + AHEAD, BUFS)) for b in range(BUFS)]

        block = ctx.enter_context(nc.Block())

        @block.sync
        def _(sp):
            sp.dma_start(craw[:, 0, :], t_in["c"][0].rearrange("(p k) -> p k", k=KT)).then_inc(s_c, 16)
            sp.dma_start(craw[:, 1, :], t_in["c_ctx"].rearrange("(p k) -> p k", k=KT)).then_inc(s_c, 16)
            for l in range(DEPTH):
                for local, key in enumerate(stream(l)):
                    s, _ = chunks.where[key]
                    n = key[2]
                    if local >= 2:
                        sp.wait_ge(slot_ready[chunks.where[stream(l)[local - 2]][0]],
                                   chunks.where[stream(l)[local - 2]][1])
                    if l and local == 2:
                        for t in range(LAYER_T[l - 1]):
                            sp.wait_ge(s_yin[t], 16 * yin_loads(l - 1, t))
                    if local >= 4:
                        before = max(i for i in range(local) if STREAM_SLOTS[i] == s)
                        sp.wait_ge(made, jobs.at[last_use(stream(l)[before])] + 1)
                    elif l:
                        sp.wait_ge(expert_free, NE * l - (s < 3))
                    if key[1] == "mod":
                        src = wmod[l][:, :, n * 512:(n + 1) * 512]
                    elif key[1] == "win":
                        src = win[l][:, :, WIN[n][0]:WIN[n][1]]
                    else:
                        src = wout[l][:, 4 * (1 - n):4 * (1 - n) + 4, :]
                    sp.dma_start(slot_view(key), src).then_inc(slot_ready[s], 16)
                for e in range(2):
                    for c in range(3):
                        if e == 0 and c == 2:
                            sp.wait_ge(s_hd, 16 * (l + 1))
                        if e == 1 and c == 0:
                            sp.wait_ge(m_gath[0], 16 * (GATHERS[0] * l + 1))
                        s = 3 * e + c
                        if s < 4:
                            key = [k for k in stream(l) if chunks.where[k][0] == s][-1]
                            sp.wait_ge(made, jobs.at[last_use(key)] + 1)
                        else:
                            sp.wait_ge(made, jobs.at[(l, "out", LAYER_T[l] - 1, 1)] + 1)
                        src = ewout[NE * l + e] if c == 2 else ewin[NE * l + e, c]
                        sp.dma_start(slot[s], src).then_inc(slot_ready[s], 16)
                with sp.Fori(1, NE // 2) as pair:
                    e0 = pair * 2
                    for par in range(2):
                        sp.wait_ge(expert_free, e0 + (NE * l + par - 1))
                        sp.sem_inc(s_paced, 1)
                        for c in range(3):
                            if c == 2:
                                s, v = chunks.where[(l, "expert", par, 0)]
                            else:
                                s, v = chunks.where[(l, "expert", 1 - par, c + 1)]
                                v -= 16 * (1 - par)
                            sp.wait_ge(slot_ready[s], pair * 16 + v)
                            sp.sem_inc(s_paced, 1)
                            if c == 2:
                                src = ewout[bass.ds(e0 + (NE * l + par), 1), :, :].rearrange("o p n -> (o p) n")
                            else:
                                src = ewin[bass.ds(e0 + (NE * l + par), 1), c, :, :].rearrange("o p n -> (o p) n")
                            sp.dma_start(slot[3 * par + c], src).then_inc(slot_ready[3 * par + c], 16)
            for t in range(XT_TILES):
                sp.wait_ge(s_fin, t + 1)
                sp.dma_start(out[0, t * P:(t + 1) * P, :], X[:, t, :]).then_inc(s_out, 16)
            sp.wait_ge(s_out, 16 * XT_TILES)

        @block.gpsimd
        def _(pool):
            steps = [0]

            def link(ins):
                steps[0] += 1
                ins.then_inc(s_pool, 1)
                pool.wait_ge(s_pool, steps[0])

            pool.memset(csil[:, :, :], 0.0).then_inc(s_setup, 1)
            pool.memset(poolw[:, :, :], 0.0).then_inc(s_setup, 1)
            pool.memset(wgate[:, :], 0.0).then_inc(s_setup, 1)
            pool.memset(zT[:, :], 1.0).then_inc(s_setup, 1)
            for b in range(BUFS):
                pool.dma_start(spare[:, b:b + 1], t_in["c"][0, P * b:P * (b + 1)].rearrange("(p o) -> p o", o=1)) \
                    .then_inc(m_scat[b], 16)
            for l in range(DEPTH):
                nt = LAYER_T[l]
                vs = 2 if l < DEPTH - 1 else 1

                def store_gates(i):
                    g = i // 5
                    got(pool, "D", l, "modT", i)
                    row = 2 * (2 * l + g)
                    pool.dma_start(gd[row:row + 2, :].rearrange("v (p k) -> p v k", k=KT),
                                   gvec[:, g, :, :]).then_inc(s_gs, 16)

                def load_gates(i):
                    g = i // 5
                    pool.wait_ge(s_gs, 16 * (2 * l + g + 1))
                    row = 2 * (2 * l + g)
                    pool.dma_start(gates[:, 0:vs, :], bc(gd[row:row + vs, :], 0, P)).then_inc(s_gb, 16)

                if l:
                    pool.wait_ge(s_comb, sum(LAYER_T[:l]))
                pool.memset(pin[:, :, :], 0.0).then_inc(s_setup, 1)
                pool.memset(S0, 0.0).then_inc(s_setup, 1)
                n = POOL_N if nt == TILES else POOL_X
                for m in range(2):
                    got(pool, "A", l, "pool", m)
                    a, b, src = pA, pB, pin[:, m, :]
                    inv = const("inv").rearrange("p (m n) -> p m n", m=2)[:, m, :]
                    link(pool.tensor_tensor(a[:, 1:n], src[:, 0:n - 1], src[:, 1:n], ALU.add))
                    link(pool.tensor_tensor(b[:, 2:n - 1], a[:, 1:n - 2], a[:, 3:n], ALU.add))
                    if m == 1:
                        link(pool.tensor_tensor(a[:, 4:n - 3], b[:, 2:n - 5], b[:, 6:n - 1], ALU.add))
                        link(pool.tensor_tensor(b[:, 8:n - 7], a[:, 4:n - 11], a[:, 12:n - 3], ALU.add))
                    for q in range(2 if nt == TILES else 1):
                        for h, s in ((0, a), (1, b)):
                            ph = slice(64 * h, 64 * h + 64)

                            def mid(z):
                                if q:
                                    return z[ph, POOL_X + PADW:POOL_X + PADW + CTX]
                                return z[ph, 0:POOL_X].rearrange("p (r w) -> p r w", r=ROWS)[:, :, PADW:PADW + GRID_W]

                            link(pool.tensor_tensor(mid(s), mid(s), mid(inv), ALU.mult))
                            link(pool.tensor_tensor(mid(src), mid(s), mid(src), ALU.subtract))
                    pool.sem_inc(s_pdiff, 1)
                for t in range(nt):
                    for d in range(2):
                        if t:
                            pool.wait_ge(made, jobs.at[(l, "score", t - 1, d)] + 1)
                        got(pool, "A", l, "tq", d)
                        pool.tensor_tensor(qbd[:, d, :].rearrange("p (h i) -> p h i", h=HEADS),
                                           bc(qdT[:, d, t * P:(t + 1) * P], 1, HEADS), bc(const("heads"), 2, P),
                                           ALU.mult).then_inc(s_qbd, 1)
                    if t == 0:
                        store_gates(2)
                    if t == min(2, nt - 1):
                        load_gates(2)
                pool.wait_ge(made, jobs.at[(l, "router")] + 1)
                pool.iota(iota, pattern=[[1, 512]], base=0, channel_multiplier=0,
                          allow_small_or_imprecise_dtypes=True).then_inc(s_iota, 1)
                pool.wait_ge(s_res, sum(LAYER_T[:l + 1]))
                pool.wait_ge(made, jobs.at[(l, "slots")] + 1)
                pool.memset(xg[:, :, :], 0.0).then_inc(s_pool, 1)
                pool.memset(xg_x, 0.0).then_inc(s_pool, 1)
                steps[0] += 2
                pool.wait_ge(s_pool, steps[0])
                got(pool, "D", l, "extra")
                pool.wait_ge(s_hd, 16 * (l + 1))
                rows_h = hd[0:2 * nt * P, :]
                rows_y = yd[0:4 * nt * P, :]
                m0 = (NE + 1) * l

                def gather(buf, e, value):
                    pool.tensor_copy(gidx[:, buf:buf + 1], gtab[:, 0, bass.ds(e, 1)]).then_inc(m_gi, 1)
                    pool.wait_ge(m_gi, value)
                    pool.sem_inc(s_mark, 1)
                    pool.indirect_dma_start(
                        out=xg[:, buf, :], out_offset=None, in_=rows_h,
                        in_offset=bass.IndirectOffsetOnAxis(ap=gidx[:, buf:buf + 1], axis=0),
                        bounds_check=2 * nt * P - 1, oob_is_err=False).then_inc(m_gath[buf], 16)

                def gather_x(b, k, e):
                    at = (b + 1) * (NE + AHEAD) + e
                    pool.tensor_copy(gidx_x[:, :], row_g[:, bass.ds(at, 1)]).then_inc(x_idx[l], 1)
                    pool.tensor_copy(sidx_x[:, :], row_s[:, bass.ds(at, 1)]).then_inc(x_idx[l], 1)
                    pool.wait_ge(x_idx[l], k * 2 + 2)
                    pool.sem_inc(s_mark, 1)
                    pool.indirect_dma_start(
                        out=xg_x, out_offset=None, in_=rows_h,
                        in_offset=bass.IndirectOffsetOnAxis(ap=gidx_x[:, :], axis=0),
                        bounds_check=2 * nt * P - 1, oob_is_err=False).then_inc(x_gath[l], 16)

                def scatter_x(k):
                    pool.wait_ge(x_y[l], k + 1)
                    pool.sem_inc(s_mark, 1)
                    pool.indirect_dma_start(
                        out=rows_y, out_offset=bass.IndirectOffsetOnAxis(ap=sidx_x[:, :], axis=0),
                        in_=ye_x, in_offset=None,
                        bounds_check=4 * nt * P - 1, oob_is_err=False).then_inc(x_scat[l], 16)
                    pool.wait_ge(x_scat[l], k * 16 + 16)
                    pool.sem_inc(s_mark, 1)

                row_g = gtab[:, :, :].rearrange("p b e -> p (b e)")
                row_s = stab[:, :, :].rearrange("p b e -> p (b e)")
                for e in range(AHEAD):
                    gather(e, e, (NE + AHEAD) * l + e + 1)
                store_gates(5)
                load_gates(5)
                with pool.Fori(0, NE // BUFS) as turn:
                    e0 = turn * BUFS
                    for i in range(BUFS):
                        pool.wait_ge(m_t1, e0 + (m0 + i + 1))
                        gather((i + AHEAD) % BUFS, e0 + (i + AHEAD), e0 + ((NE + AHEAD) * l + AHEAD + i + 1))
                        n_x = pool.value_load(xtab[0:1, bass.ds(e0 + (NE + i), 1)], min_val=0, max_val=7)
                        k0 = pool.value_load(xtab[0:1, bass.ds(e0 + i, 1)], min_val=0, max_val=16)
                        with pool.If(n_x > 0):
                            gather_x(0, k0, e0 + i)
                        pool.wait_ge(m_y, e0 + (m0 + i + 2))
                        pool.tensor_copy(sidx[:, i:i + 1], stab[:, 0, bass.ds(e0 + i, 1)]).then_inc(m_si, 1)
                        pool.wait_ge(m_si, e0 + (NE * l + i + 1))
                        pool.sem_inc(s_mark, 1)
                        pool.indirect_dma_start(
                            out=rows_y, out_offset=bass.IndirectOffsetOnAxis(ap=sidx[:, i:i + 1], axis=0),
                            in_=ye[:, i, :], in_offset=None,
                            bounds_check=4 * nt * P - 1, oob_is_err=False).then_inc(m_scat[i], 16)
                        with pool.If(n_x > 0):
                            scatter_x(k0)
                            with pool.If(n_x > 1):
                                with pool.Fori(1, n_x) as b:
                                    gather_x(b, k0 + b, e0 + i)
                                    scatter_x(k0 + b)
                for i in range(BUFS):
                    pool.wait_ge(m_scat[i], 16 * ((NE // BUFS) * (l + 1) + 1))
                for t in range(nt):
                    if t == 2:
                        pool.wait_ge(expert_free, NE * (l + 1))
                    src = yd[0:4 * nt * P, :].rearrange("(j t p h) n -> t p j (h n)", j=2, t=nt, h=2)[t]
                    pool.dma_start(yin[t], src).then_inc(s_yin[t], 16)

        @block.scalar
        def _(act):
            steps = [0]

            def link(ins):
                steps[0] += 1
                ins.then_inc(s_act, 1)
                act.wait_ge(s_act, steps[0])

            def copy(o, i, func=ACT.Copy, **kw):
                return act.activation(o, i, func, **kw)

            def load_params(l):
                n = 0

                def ld(o, i):
                    nonlocal n
                    act.dma_start(o, i).then_inc(s_par, 16)
                    n += 1

                b = t_in["b_mod"][l].rearrange("(i p k) -> p i k", p=P, k=KT)
                act.dma_start(bmod[:, :, :], b).then_inc(s_mpar, 16)
                for i in range(2):
                    src = t_in[f"g_norm{i + 1}"][l].rearrange("(p k) -> p k", k=KT)
                    act.dma_start(gnorm[:, i, :], src).then_inc(s_mpar, 16)
                row = lambda name: t_in[name][l:l + 1, :]
                ld(vecs[0:CONF_K, :], t_in["conf_w_dw"][l])
                ld(vecs[V_CB:V_CB + 1, :], row("conf_b_dw"))
                ld(vecs[V_LG:V_LG + 1, :], row("conf_ln_g"))
                ld(vecs[V_LB:V_LB + 1, :], row("conf_ln_b"))
                ld(vecs[V_SC:V_SC + SC_K, :], t_in["sc_w_dw"][l])
                ld(vecs[V_PS:V_PS + 1, :], row("pool_scale"))
                ld(wgate[0:RANK, 0:QK_W], t_in["gla_w_gate_f"][l])
                ld(wgate[RANK:2 * RANK, QK_W:2 * QK_W], t_in["gla_w_gate_b"][l])
                ld(wgate[2 * RANK:2 * RANK + 1, 0:QK_W], row("gla_b_gate_f"))
                ld(wgate[2 * RANK:2 * RANK + 1, QK_W:2 * QK_W], row("gla_b_gate_b"))
                ld(gout[:, :], row("gla_g_out").broadcast_to([P, GROUP_W]))
                for g in range(4):
                    h = 64 * (g % 2)
                    ld(poolw[h:h + 64, g // 2, h:h + 64], t_in["pool_w"][l, g])
                ld(wre[:, :, :], t_in["router_w_expert"][l].rearrange("(p k) n -> p k n", k=KT))
                ld(wrg[:, :, :], t_in["router_w_group"][l].rearrange("(p k) n -> p k n", k=KT))
                for g in (0, 64):
                    ld(rbias[g:g + NE, :], t_in["router_b_expert"][l:l + 1, :].rearrange("o n -> n o"))
                    ld(rbias[g + NE:g + NE + NG, :], t_in["router_b_group"][l:l + 1, :].rearrange("o n -> n o"))
                assert n == N_PAR, n

            act.dma_start(cst[:, :], t_in["consts"]).then_inc(s_cst, 16)
            act.dma_start(X[:, 0:XT_TILES, :], t_in["x"][0].rearrange("(t p) d -> p t d", p=P)).then_inc(s_in, 16)
            act.dma_start(X[:, XT_TILES:, :], t_in["ctx"][0].rearrange("(t p) d -> p t d", p=P)).then_inc(s_in, 16)
            act.wait_ge(s_setup, 1)
            act.wait_ge(s_c, 32)
            for v in range(2):
                act.activation(csil[:, :, v], craw[:, v, :], ACT.Silu).then_inc(s_csil, 1)
            act.wait_ge(s_setup, 4)
            load_params(0)

            def mod_rows(l, n):
                bank = take(act, l, "mod", n)
                done(copy(msb[:, n % 2, :], bank[:, :]), "A", l, "mod", n)

            def root_of_squares(l, n, t):
                if n == 1:
                    act.wait_ge(s_res, sum(LAYER_T[:l]) + t + 1)
                elif l and t < LAYER_T[l - 1]:
                    act.wait_ge(s_comb, sum(LAYER_T[:l - 1]) + t + 1)
                link(act.activation(xn[:, t, :], X[:, t, :], ACT.Square, accum_out=ss[:, t:t + 1]))
                copy(rstd[:, t:t + 1], ss[:, t:t + 1], ACT.Sqrt, bias=const("eps"), scale=1.0 / D).then_inc(s_ss, 1)

            def norm(l, n, tiles):
                outputs = LAYER_T[l - 1] if l and n == 0 else 0
                for t in range(-1 if outputs else 0, tiles + 1):
                    if t + 1 < outputs:
                        act.wait_ge(s_yin[t + 1], 16 * yin_loads(l - 1, t + 1))
                        y1 = yin[t + 1][:, 0, :]
                        copy(y1, y1, scale=wt[:, 0, t + 1:t + 2]).then_inc(s_w1, 1)
                    if 0 <= t < tiles:
                        root_of_squares(l, n, t)
                    if t >= 1 and l < DEPTH:
                        act.wait_ge(s_rstd, norm_base(l, n) + t)
                        act.activation(xn[:, t - 1, :], X[:, t - 1, :], ACT.Copy,
                                       scale=rstd[:, t - 1:t]).then_inc(s_xn, 1)

            def modulate(l, n, tiles):
                for k in range(0, KT, 2):
                    bank = take(act, l, "norm", n, k)
                    for v in range(2 if tiles == TILES else 1):
                        ins = act.activation(aT[:, k, 256 * v:256 * v + 256], bank[:, 256 * v:256 * v + 256],
                                             ACT.Identity, bias=modv[:, n, 0, v, k:k + 1],
                                             scale=modv[:, n, 1, v, k:k + 1])
                    done(ins, "A", l, "norm", n, k)

            for l in range(DEPTH):
                nt = LAYER_T[l]
                N = nt * P
                vs = 2 if l < DEPTH - 1 else 1
                n_y = sum(LAYER_T[:l])
                if l == 0:
                    act.wait_ge(s_cst, 16)
                    act.wait_ge(s_in, 32)
                else:
                    mod_rows(l, 0)
                    mod_rows(l, 1)
                norm(l, 0, TILES)
                for n in range(0 if l == 0 else 2, 4):
                    mod_rows(l, n)
                act.wait_ge(s_modv, 2 * l + 1)
                modulate(l, 0, TILES)
                for m in range(2):
                    bank = take(act, l, "cgate", m)
                    done(copy(sg[:, m, 0:N], bank[:, 0:N], ACT.Sigmoid), "A", l, "cgate", m)
                for m in range(2):
                    bank = take(act, l, "scb", m)
                    done(copy(scb[:, m, 0:N], bank[:, 0:N]), "A", l, "scb", m)
                for m in range(2):
                    bank = take(act, l, "scc", m)
                    done(copy(scc[:, m, 0:N], bank[:, 0:N]), "A", l, "scc", m)
                act.wait_ge(s_setup, 4 + 2 * (l + 1))
                for m in range(2):
                    bank = take(act, l, "pool", m)
                    ins = copy(pin[:, m, 0:POOL_X].rearrange("p (r w) -> p r w", r=ROWS)[:, :, PADW:PADW + GRID_W],
                               bank[:, 0:SEQ].rearrange("p (r w) -> p r w", r=ROWS))
                    if nt == TILES:
                        ins = copy(pin[:, m, POOL_X + PADW:POOL_X + PADW + CTX], bank[:, SEQ:SEQ + CTX])
                    done(ins, "A", l, "pool", m)
                bank = take(act, l, "z")
                for t in range(TILES):
                    ins = copy(zT[0:2 * RANK, t * P:(t + 1) * P], bank[2 * RANK * t:2 * RANK * (t + 1), 0:P])
                done(ins, "A", l, "z")
                for i in range(2):
                    bank = take(act, l, "zw", i)
                    o = lab[:, :, 2 * i:2 * i + 2, :].rearrange("p d t c -> p t d c")
                    ins = copy(o, bank[:, :].rearrange("p (t d c) -> p t d c", t=2, d=2), ACT.Abs)
                    done(ins, "A", l, "zw", i)
                got(act, "A", l, "zw", 1)
                flat = lab.rearrange("p d t c -> p (d t c)")
                link(copy(flat, flat, ACT.Exp, scale=-1.0))
                copy(flat, flat, ACT.Ln, bias=1.0).then_inc(s_lab, 1)
                got(act, "D", l, "mean")
                copy(sg[:, :, 0:N], glu[:, :, 0:N], ACT.Square).then_inc(s_sq, 1)
                for t in range(nt):
                    bank = take(act, l, "g", t)
                    done(copy(qkvg[:, t, 512:768], bank[:, 0:256], ACT.Silu), "A", l, "g", t)
                bank = take(act, l, "var")
                done(copy(u[:, 0, 0:N], bank[:, 0:N], ACT.Sqrt, bias=const("eps"), scale=1.0 / GROUP_W), "A", l, "var")
                for i, outs in enumerate((((0, 1.0), (1, -1.0)), ((2, 1.0),), ((3, 1.0), (4, -1.0)), ((5, 1.0),))):
                    bank = take(act, l, "cum", i)
                    for j, s in outs:
                        ins = copy(ex[:, j, :, :].rearrange("p t c -> p (t c)"), bank[:, :], ACT.Exp,
                                   scale=s / GATE_NORM)
                    done(ins, "A", l, "cum", i)
                bank = take(act, l, "dec")
                ins = copy(dec, bank[:, 0:2 * NCH].rearrange("p (i c) -> p i c", i=2), ACT.Exp, scale=1 / GATE_NORM)
                done(ins, "A", l, "dec")
                for t in range(TILES):
                    bank = take(act, l, "qkv", t)
                    a = 0 if t < nt else QK_W
                    done(copy(qkvg[:, t, a:512], bank[:, a:512]), "A", l, "qkv", t)
                    if t == 0:
                        act.wait_ge(s_un, l + 1)
                        for m in range(2):
                            copy(glu[:, m, 0:N], glu[:, m, 0:N], ACT.Silu, bias=chv[:, m, V_LB:V_LB + 1],
                                 scale=chv[:, m, V_LG:V_LG + 1]).then_inc(s_yc, 1)
                mod_rows(l, 4)
                mod_rows(l, 5)
                for d in range(2):
                    bank = take(act, l, "tq", d)
                    done(copy(qdT[:, d, :], bank[:, :]), "A", l, "tq", d)
                    bank = take(act, l, "tk", d)
                    done(copy(kiT[:, d, :], bank[:, :]), "A", l, "tk", d)

                def rows_T(t):
                    bank = take(act, l, "ty", t)
                    ins = copy(aT[:, 0:2, t * P:(t + 1) * P], bank[:, 0:256].rearrange("p (m n) -> p m n", m=2))
                    done(ins, "A", l, "ty", t)

                def squares(t):
                    bank = take(act, l, "o", t)
                    sq = ex[:, t % 2, 0:2, :].rearrange("p t c -> p (t c)")
                    if t >= 2:
                        act.wait_ge(s_y, sum(LAYER_T[:l]) + t - 1)
                    done(copy(sq, bank[:, 0:256], ACT.Square), "A", l, "o", t)
                    act.wait_ge(s_so, n_y + t + 1)
                    so = sso[:, HEADS * t:HEADS * (t + 1)]
                    copy(so, so, ACT.Sqrt, bias=const("eps"), scale=1.0 / DV).then_inc(s_ro, 1)

                stages = {"o": squares, "ty": rows_T, "mod": lambda n: mod_rows(l, n)}
                for k in gla_steps(l)[:-2]:
                    if k[0] in stages:
                        stages[k[0]](k[1])
                norm(l, 1, nt)
                mod_rows(l, 10)
                mod_rows(l, 11)
                act.wait_ge(s_modv, 2 * l + 2)
                modulate(l, 1, nt)
                bank = take(act, l, "router")
                for g in range(2):
                    rows = slice(64 * g, 64 * g + NE + NG)
                    ins = copy(lgT[0:NE + NG, N // 2 * g:N // 2 * (g + 1)], bank[rows, 0:N // 2], ACT.Identity,
                               bias=rbias[rows, :])
                done(ins, "A", l, "router")
                for t in range(nt):
                    for h in range(2):
                        bank = take(act, l, "htok", t, h)
                        done(copy(htok[:, t, HALF * h:HALF * (h + 1)], bank[:, :]), "A", l, "htok", t, h)
                got(act, "A", l, "htok", nt - 1, 1)
                dst = hd[0:2 * nt * P, :].rearrange("(t p h) n -> p t (h n)", t=nt, h=2)
                act.dma_start(dst, htok[:, 0:nt, :]).then_inc(s_hd, 16)
                act.wait_ge(s_ddh, 2 * l + 1)
                copy(r4[1][:, 0:nt, :], r4[0][:, 0:nt, :], ACT.Exp).then_inc(s_eg, 1)
                act.wait_ge(s_ddh, 2 * l + 2)
                copy(rr[3][:, 0:nt], rr[2][:, 0:nt], ACT.Exp).then_inc(s_eg, 1)
                got(act, "D", l, "extra")
                got(act, "D", l, "modT", 5)
                if l + 1 < DEPTH:
                    load_params(l + 1)

                def hidden(bank, r, made_sem, value, up):
                    act.wait_ge(made_sem, value)
                    copy(r, bank[:, :]).then_inc(up, 1)

                def silu(bank, s, made_sem, value, up):
                    act.wait_ge(made_sem, value)
                    copy(s, bank[:, :].rearrange("p (k n) -> p k n", k=4)[:, :, 0:BLK], ACT.Silu).then_inc(up, 1)

                with act.Fori(0, NE // BUFS) as turn:
                    e0 = turn * BUFS
                    for i in range(BUFS):
                        par = i % 2
                        n = NE * l + i + 1
                        hidden(PS[1], raw, m_g1, e0 + n, m_raw)
                        silu(PS[2], sil, m_t2, e0 + n, m_sil)
                        n_x = act.value_load(xtab[0:1, bass.ds(e0 + (NE + i), 1)], min_val=0, max_val=7)
                        k0 = act.value_load(xtab[0:1, bass.ds(e0 + i, 1)], min_val=0, max_val=16)
                        with act.If(n_x > 0):
                            with act.Fori(0, n_x) as b:
                                k = k0 + b
                                hidden(PS[5], raw_x, x_g1[l], k + 1, x_raw[l])
                                silu(PS[6], sil_x, x_t2[l], k + 1, x_sil[l])
            act.dma_start(gfin, t_in["g_final"].rearrange("(o d) -> o d", o=1).broadcast_to([P, D])).then_inc(s_gf, 16)
            norm(DEPTH, 0, XT_TILES)

        @block.tensor
        def _(pe):
            mm = pe.matmul
            tr = pe.transpose
            freed = {"A": 0, "D": 0}

            def open_(l, *key):
                i = jobs.at[(l,) + key]
                assert i == jobs.next, (key, jobs.keys[jobs.next])
                jobs.next += 1
                if i >= 8:
                    for c in jobs.readers[i - 8]:
                        if jobs.upto[i - 8][c] > freed[c]:
                            freed[c] = jobs.upto[i - 8][c]
                            pe.wait_ge(read_a if c == "A" else read_d, freed[c])
                return PS[i % 8]

            def chunk(l, *key):
                s, v = chunks.where[(l,) + key]
                pe.wait_ge(slot_ready[s], v)
                return slot_view((l,) + key)

            pe.wait_ge(s_csil, 2)

            def mod_product(l, n):
                w = chunk(l, "mod", n)
                bank = open_(l, "mod", n)
                for k in range(KT):
                    g = 32 * (k % 4)
                    ins = mm(bank[g:g + 32, :], csil[:, k, :], w[:, k, :], start=k < 4, stop=k >= 4)
                ins.then_inc(made, 1)

            def mod_T(l, i):
                got(pe, "A", l, "mod", 2 * i + 1)
                bank = open_(l, "modT", i)
                for h in range(2):
                    rows = msb[:, h, :].rearrange("p (q k) -> p k q", k=KT)
                    for k in range(KT):
                        ins = mm(bank[64 * h:64 * h + 64, 2 * k:2 * k + 2], rows[:, k, :], const("sel"),
                                 start=True, stop=True)
                ins.then_inc(made, 1)

            def norm_T(l, n, tiles):
                pe.wait_ge(s_xn, sum(TILES + LAYER_T[i] for i in range(l)) + TILES * n + tiles)
                for k in range(KT):
                    bank = open_(l, "norm", n, k)
                    for t in range(tiles):
                        v = xn[:, t, :].rearrange("p (q k) -> p k q", k=KT)[:, k, :]
                        ins = tr(bank[:, t * P:(t + 1) * P], v, ident)
                    ins.then_inc(made, 1)

            for l in range(DEPTH):
                nt = LAYER_T[l]
                N = nt * P
                for i in range(2):
                    mod_product(l, 2 * i)
                    mod_product(l, 2 * i + 1)
                    if l == i == 0:
                        pe.wait_ge(s_cst, 16)
                    mod_T(l, i)
                pe.wait_ge(s_par, 16 * N_PAR * (l + 1))
                bank = open_(l, "vec")
                for m in range(2):
                    ins = tr(bank[:, VEC_ROWS * m:VEC_ROWS * (m + 1)], vecs[0:VEC_ROWS, m * P:(m + 1) * P],
                             ident[0:VEC_ROWS, 0:VEC_ROWS])
                ins.then_inc(made, 1)
                norm_T(l, 0, TILES)
                got(pe, "A", l, "norm", 0, KT - 2)
                got(pe, "D", l, "norm", 0, KT - 1)

                def channels(w, m, *key):
                    bank = open_(l, *key)
                    for k in range(KT):
                        ins = mm(bank[:, 0:N], w[:, k, m * P:(m + 1) * P], aT[:, k, 0:N], start=k == 0,
                                 stop=k == KT - 1)
                    return ins.then_inc(made, 1)

                w = chunk(l, "win", 0)
                for m in range(2):
                    channels(w, 2 + m, "cgate", m)
                    ins = channels(w, m, "ca", m)
                w = chunk(l, "win", 1)
                for name, a in (("scb", 0), ("scc", 2)):
                    for m in range(2):
                        ins = channels(w, a + m, name, m)
                w = chunk(l, "win", 2)
                for name, a in (("scx", 0), ("pool", 2)):
                    for m in range(2):
                        ins = channels(w, a + m, name, m)
                w = chunk(l, "win", 4)
                bank = open_(l, "z")
                for k in range(KT):
                    for t in range(TILES):
                        ins = mm(bank[2 * RANK * t:2 * RANK * (t + 1), 0:P], w[:, k, 256:288],
                                 aT[:, k, t * P:(t + 1) * P], start=k == 0, stop=k == KT - 1)
                ins.then_inc(made, 1)
                got(pe, "A", l, "z")
                for i in range(2):
                    bank = open_(l, "zw", i)
                    for t in range(2):
                        a = (2 * i + t) * P
                        ins = mm(bank[:, 256 * t:256 * t + 256], zT[0:2 * RANK + 1, a:a + P],
                                 wgate[0:2 * RANK + 1, :], start=True, stop=True)
                    ins.then_inc(made, 1)
                pe.wait_ge(s_u, l + 1)
                bank = open_(l, "mean")
                for m in range(2):
                    ins = mm(bank[:, 0:N], ones, u[:, m, 0:N], start=m == 0, stop=m == 1)
                ins.then_inc(made, 1)
                for t in range(nt):
                    bank = open_(l, "g", t)
                    for k in range(KT):
                        ins = mm(bank[:, 0:256], aT[:, k, t * P:(t + 1) * P], w[:, k, 0:256], start=k == 0,
                                 stop=k == KT - 1)
                    ins.then_inc(made, 1)
                pe.wait_ge(s_sq, l + 1)
                bank = open_(l, "var")
                for m in range(2):
                    ins = mm(bank[:, 0:N], ones, sg[:, m, 0:N], start=m == 0, stop=m == 1)
                ins.then_inc(made, 1)
                got(pe, "D", l, "zw", 1)
                for i, name in enumerate(("cum_f", "after", "cum_b", "prev")):
                    bank = open_(l, "cum", i)
                    mm(bank[:, :], const(name), la[:, i // 2, :, :].rearrange("p t c -> p (t c)"), start=True,
                       stop=True).then_inc(made, 1)
                bank = open_(l, "dec")
                for d in range(2):
                    for t in range(TILES):
                        a = 2 * (TILES * d + t)
                        ins = mm(bank[:, a:a + 2], la[:, d, t, :], const("chunks"), start=True, stop=True)
                ins.then_inc(made, 1)
                w = chunk(l, "win", 3)
                for t in range(TILES):
                    bank = open_(l, "qkv", t)
                    a = 0 if t < nt else QK_W
                    for k in range(KT):
                        ins = mm(bank[:, a:512], aT[:, k, t * P:(t + 1) * P], w[:, k, a:512], start=k == 0,
                                 stop=k == KT - 1)
                    ins.then_inc(made, 1)
                    if t:
                        continue
                    pe.wait_ge(s_pdiff, 2 * (l + 1))
                    for m in range(2):
                        bank = open_(l, "pm", m)
                        rows = pin[:, m, 0:POOL_X].rearrange("p (r w) -> p r w", r=ROWS)[:, :, PADW:PADW + GRID_W]
                        ins = mm(bank[:, 0:SEQ], poolw[:, m, :], rows, start=True, stop=True)
                        if nt == TILES:
                            ins = mm(bank[:, SEQ:SEQ + CTX], poolw[:, m, :],
                                     pin[:, m, POOL_X + PADW:POOL_X + PADW + CTX], start=True, stop=True)
                        ins.then_inc(made, 1)
                mod_product(l, 4)
                mod_product(l, 5)
                for d in range(2):
                    if d:
                        mod_T(l, 2)
                    pe.wait_ge(s_qd, 2 * l + d + 1)
                    for name, j in (("tq", 0), ("tk", 1)):
                        bank = open_(l, name, d)
                        for t in range(TILES):
                            ins = tr(bank[:, t * P:(t + 1) * P], ex[:, 3 * d + j, t, :], ident)
                        ins.then_inc(made, 1)
                for t in (2, 3, 0, 1):
                    for par in range(2):
                        bank = open_(l, "kv", t, par)
                        ph = slice(64 * par, 64 * par + 64)
                        for d in range(2):
                            ins = mm(bank[:, 256 * d:256 * d + 256], ex[ph, 3 * d + 2, t, :],
                                     qkvg[ph, t, 256:512], start=True, stop=True)
                        ins.then_inc(made, 1)
                got(pe, "A", l, "tk", 1)
                n_y = sum(LAYER_T[:l])

                def rows_T(t):
                    pe.wait_ge(s_y, n_y + t + 1)
                    bank = open_(l, "ty", t)
                    for m in range(2):
                        ins = tr(bank[:, m * P:(m + 1) * P], qkvg[:, t, 512 + m * P:640 + m * P], ident)
                    ins.then_inc(made, 1)

                def scores(t):
                    for d in range(2):
                        pe.wait_ge(s_qbd, 2 * (n_y + t) + d + 1)
                        bank = open_(l, "score", t, d)
                        mm(bank[:, :], kiT[:, d, t * P:(t + 1) * P], qbd[:, d, :], start=True,
                           stop=True).then_inc(made, 1)

                def outputs(t):
                    if t == 0:
                        pe.wait_ge(s_S, l + 1)
                    bank = open_(l, "o", t)
                    for d in range(2):
                        for par in range(2):
                            a = t * P + 64 * par
                            mm(bank[64 * par:64 * par + 64, 0:256], qdT[:, d, a:a + 64],
                               state_in(d, 2 * t + par), start=d == 0, stop=False, skip_group_check=True)
                    for d in range(2):
                        got(pe, "D", l, "score", t, d)
                        for h in range(HEADS):
                            ins = mm(bank[:, DV * h:DV * (h + 1)], scm[:, d, h * P:(h + 1) * P],
                                     qkvg[:, t, 256 + DV * h:256 + DV * (h + 1)], start=False,
                                     stop=d == 1, skip_group_check=True)
                    ins.then_inc(made, 1)

                branch = [aT[:, 0, :], aT[:, 1, :], glu[:, 0, :], glu[:, 1, :], sca[:, 0, :], sca[:, 1, :],
                          u[:, 0, :], u[:, 1, :]]

                def project(t, h):
                    wa, wb = chunk(l, "wout", 0), chunk(l, "wout", 1)
                    if t == h == 0:
                        got(pe, "D", l, "pm", 1)
                        pe.wait_ge(s_yc, 2 * (l + 1))
                    got(pe, "A", l, "ty", t)
                    bank = open_(l, "out", t, h)
                    for j, k in enumerate((4, 5, 6, 7, 0, 1, 2, 3)):
                        w = wa if k >= 4 else wb
                        ins = mm(bank[:, :], branch[k][:, t * P:(t + 1) * P], w[:, k % 4, 512 * h:512 * h + 512],
                                 start=j == 0, stop=j == KT - 1)
                    ins.then_inc(made, 1)

                stages = {"scores": scores, "o": outputs, "ty": rows_T, "out": project,
                          "mod": lambda n: mod_product(l, n), "modT": lambda i: mod_T(l, i)}
                for name, *args in gla_steps(l):
                    stages[name](*args)
                norm_T(l, 1, nt)
                got(pe, "A", l, "norm", 1, KT - 2)
                got(pe, "D", l, "norm", 1, KT - 1)
                bank = open_(l, "router")
                for k in range(KT):
                    for g in range(2):
                        ins = mm(bank[64 * g:64 * g + NE + NG, 0:N // 2], wrt[:, k, :],
                                 aT[:, k, N // 2 * g:N // 2 * (g + 1)], start=k == 0, stop=k == KT - 1)
                ins.then_inc(made, 1)
                got(pe, "A", l, "router")
                bank = open_(l, "routerT")
                for t in range(nt):
                    ins = tr(bank[:, t * (NE + NG):(t + 1) * (NE + NG)], lgT[0:NE + NG, t * P:(t + 1) * P],
                             ident[0:NE + NG, 0:NE + NG])
                ins.then_inc(made, 1)
                for t in range(nt):
                    for h in range(2):
                        bank = open_(l, "htok", t, h)
                        for k in range(4):
                            ins = tr(bank[:, k * P:(k + 1) * P], aT[:, 4 * h + k, t * P:(t + 1) * P], ident)
                        ins.then_inc(made, 1)
                pe.wait_ge(s_M, l + 1)
                M = l32[5]
                bank = open_(l, "pos")
                for t in range(nt):
                    for s in range(t + 1):
                        ins = mm(bank[:, t * NE:(t + 1) * NE], const("before") if s == t else ones, M[:, s, :],
                                 start=s == 0, stop=s == t)
                ins.then_inc(made, 1)
                bank = open_(l, "cnt")
                for t in range(nt):
                    ins = mm(bank[0:NE, 0:1], M[:, t, :], ones[:, 0:1], start=t == 0, stop=t == nt - 1)
                ins.then_inc(made, 1)
                bank = open_(l, "slots")
                for i in range(2 * nt):
                    pe.wait_ge(s_oneh, 2 * sum(LAYER_T[:l]) + i + 1)
                    for b in range(2 * nt):
                        for w in range(2):
                            ins = mm(bank[BLK * w:BLK * (w + 1), 2 * NE * b:2 * NE * (b + 1)],
                                     oneh[:, i, BLK * b:BLK * (b + 1)], rhs[i // nt][:, i % nt, :],
                                     start=i == b == 0, stop=i == 2 * nt - 1, skip_group_check=True)
                ins.then_inc(made, 1)
                pe.wait_ge(s_nb, l + 1)
                bank = open_(l, "extra")
                mm(bank[0:1, 0:NE], cnt[0:NE, 8:9], const("before", NE)[:, 0:NE], start=True, stop=True)
                mm(bank[0:1, NE:2 * NE], cnt[0:NE, 8:9], const("ident", NE)[:, 0:NE], start=True,
                   stop=True).then_inc(made, 1)
                mod_T(l, 5)
                for c, s in (("A", read_a), ("D", read_d)):
                    pe.wait_ge(s, jobs.upto[jobs.next - 1][c])
                    freed[c] = jobs.upto[jobs.next - 1][c]
                got(pe, "D", l, "extra")

                m0 = (NE + 1) * l
                base = [chunks.where[(l, "expert", e, c)][1] for e in range(2) for c in range(3)]

                def tokens_T(bank, x, up):
                    for k in range(4):
                        ins = tr(bank[:, k * P:(k + 1) * P], x[:, k * P:(k + 1) * P], ident)
                    ins.then_inc(up, 1)

                def hidden(bank, xT, par, up, e0=None):
                    for h in range(2):
                        if e0 is not None:
                            pe.wait_ge(slot_ready[3 * par + h], e0[0] * 8 + (base[3 * par + h] + 16 * (e0[1] // 2)))
                        w = slot[3 * par + h].rearrange("p (k n) -> p k n", k=4)
                        for k in range(4):
                            for g in range(2):
                                ins = mm(bank[64 * g:64 * g + 64, :], xT[:, k, BLK * h:BLK * (h + 1)],
                                         w[:, k, 512 * g:512 * g + 512], start=h == 0 and k == 0,
                                         stop=h == 1 and k == 3)
                    ins.then_inc(up, 1)

                def hidden_T(bank, r, up):
                    v = r.rearrange("p (q k) -> p k q", k=4)
                    for k in range(4):
                        ins = tr(bank[:, k * P:(k + 1) * P], v[:, k, :], ident)
                    ins.then_inc(up, 1)

                def back(bank, h_, par, up):
                    w = slot[3 * par + 2].rearrange("p (k n) -> p k n", k=4)
                    for k in range(4):
                        for g in range(2):
                            ins = mm(bank[64 * g:64 * g + 64, :], h_[:, k, :], w[:, k, 512 * g:512 * g + 512],
                                     start=k == 0, stop=k == 3)
                    ins.then_inc(up, 1)

                pe.wait_ge(m_gath[0], 16 * (GATHERS[0] * l + 1))
                tokens_T(PS[0], xg[:, 0, :], m_t1)
                with pe.Fori(0, NE // BUFS) as turn:
                    e0 = turn * BUFS
                    for i in range(BUFS):
                        par = i % 2
                        n = NE * l + i + 1
                        pe.wait_ge(m_xeT, e0 + (m0 + i + 1))
                        hidden(PS[1], xeT[:, par, :, :], par, m_g1, (e0, i))
                        b1 = (i + 1) % BUFS
                        pe.wait_ge(m_gath[b1], turn * 16 + (16 * (GATHERS[b1] * l + 1 + (i + 1) // BUFS)))
                        tokens_T(PS[0], xg[:, b1, :], m_t1)
                        pe.wait_ge(m_raw, e0 + n)
                        hidden_T(PS[2], raw, m_t2)
                        pe.wait_ge(m_hT, e0 + n)
                        pe.wait_ge(m_y, e0 + (m0 + i + 1))
                        pe.wait_ge(slot_ready[3 * par + 2], e0 * 8 + (base[3 * par + 2] + 16 * (i // 2)))
                        back(PS[3], hT, par, m_g2)
                        n_x = pe.value_load(xtab[0:1, bass.ds(e0 + (NE + i), 1)], min_val=0, max_val=7)
                        k0 = pe.value_load(xtab[0:1, bass.ds(e0 + i, 1)], min_val=0, max_val=16)
                        with pe.If(n_x > 0):
                            with pe.Fori(0, n_x) as b:
                                k = k0 + b
                                pe.wait_ge(x_gath[l], k * 16 + 16)
                                tokens_T(PS[4], xg_x, x_t1[l])
                                pe.wait_ge(x_xeT[l], k + 1)
                                hidden(PS[5], xeT_x, par, x_g1[l])
                                pe.wait_ge(x_raw[l], k + 1)
                                hidden_T(PS[6], raw_x, x_t2[l])
                                pe.wait_ge(x_hT[l], k + 1)
                                back(PS[7], hT_x, par, x_g2[l])
                                pe.wait_ge(x_y[l], k + 1)
                        pe.wait_ge(m_g2, e0 + n)
                        pe.sem_inc(expert_free, 1)
                pe.wait_ge(m_y, m0 + NE + 1)
                pe.wait_ge(m_xeT, m0 + NE + 1)

        @block.vector
        def _(dve):
            steps = [0]

            def step(ins):
                steps[0] += 1
                ins.then_inc(s_dve, 1)
                return steps[0]

            def link(ins):
                dve.wait_ge(s_dve, step(ins))

            tt = dve.tensor_tensor
            ts = dve.tensor_scalar
            stt = dve.scalar_tensor_tensor

            def invert_rms(l, n, t):
                dve.wait_ge(s_ss, norm_base(l, n) + t + 1)
                dve.reciprocal(rstd[:, t:t + 1], rstd[:, t:t + 1]).then_inc(s_rstd, 1)

            def combine(l, t):
                dve.wait_ge(s_w1, sum(LAYER_T[:l]) + t + 1)
                if t == 0:
                    dve.wait_ge(s_gb, 16 * GATE_LOADS[l, 5])
                y1, y2 = yin[t][:, 0, :], yin[t][:, 1, :]
                link(stt(y1, y2, wt[:, 1, t:t + 1], y1, ALU.mult, ALU.add))
                link(tt(y1, y1, gates[:, t // XT_TILES, :], ALU.mult))
                tt(X[:, t, :], X[:, t, :], y1, ALU.add).then_inc(s_comb, 1)

            def shift_scale(l, i):
                n, what = (0, i) if i < 2 else (1, i - 3)
                bank = take(dve, l, "modT", i)
                m = bank[:, 0:2 * KT].rearrange("p (k v) -> p v k", v=2)
                b = bc(bmod[:, i, :], 1, 2)
                if i in (2, 5):
                    done(tt(gvec[:, i // 5, :, :], m, b, ALU.add), "D", l, "modT", i)
                    return
                if what == 0:
                    done(tt(modv[:, n, 0, :, :], m, b, ALU.add), "D", l, "modT", i)
                else:
                    ins = tt(mt, m, b, ALU.add)
                    done(ins, "D", l, "modT", i)
                    got(dve, "D", l, "modT", i)
                    stt(modv[:, n, 1, :, :], mt, 1.0, bc(gnorm[:, n, :], 1, 2), ALU.add,
                        ALU.mult).then_inc(s_modv, 1)

            def modulate(l, n, tiles):
                for k in range(1, KT, 2):
                    bank = take(dve, l, "norm", n, k)
                    for v in range(2 if tiles == TILES else 1):
                        c = slice(256 * v, 256 * v + 256)
                        ins = ts(aT[:, k, c], bank[:, c], modv[:, n, 1, v, k:k + 1], modv[:, n, 0, v, k:k + 1],
                                 ALU.mult, ALU.add)
                    done(ins, "D", l, "norm", n, k)

            def taps(dst, src, m, row, width, both, bias):
                c = width // 2

                def part(kind):
                    for o in [0] + [s * a for a in range(1, c + 1) for s in (-1, 1)]:
                        w = chv[:, m, row + c + o:row + c + o + 1]
                        if kind == "across":
                            if abs(o) >= GRID_W:
                                continue
                            a, b = max(0, -o), GRID_W - max(0, o)
                            v = lambda z, d: z[:, m, 0:SEQ].rearrange("p (r w) -> p r w", r=ROWS)[:, :, a + d:b + d]
                        elif kind == "down":
                            if abs(o) >= ROWS:
                                continue
                            a, b = max(0, -o) * GRID_W, (ROWS - max(0, o)) * GRID_W
                            v = lambda z, d: z[:, m, a + d * GRID_W:b + d * GRID_W]
                        else:
                            a, b = SEQ + max(0, -o), SEQ + CTX - max(0, o)
                            v = lambda z, d: z[:, m, a + d:b + d]
                        if o == 0 and bias is not None:
                            yield lambda v=v, w=w: ts(v(dst, 0), v(src, 0), w, bias, ALU.mult, ALU.add)
                        elif o == 0:
                            yield lambda v=v, w=w: ts(v(dst, 0), v(src, 0), w, None, ALU.mult)
                        else:
                            yield lambda v=v, w=w, o=o: stt(v(dst, 0), v(src, o), w, v(dst, 0), ALU.mult, ALU.add)

                return [part("down" if m else "across")] + ([part("context")] if both else [])

            def run_chains(chains):
                last = [0] * len(chains)
                live = list(range(len(chains)))
                while live:
                    for i in list(live):
                        f = next(chains[i], None)
                        if f is None:
                            live.remove(i)
                            continue
                        if last[i]:
                            dve.wait_ge(s_dve, last[i])
                        last[i] = step(f())
                dve.wait_ge(s_dve, steps[0])

            for l in range(DEPTH):
                nt = LAYER_T[l]
                N = nt * P
                vs = 2 if l < DEPTH - 1 else 1
                n_y = sum(LAYER_T[:l])
                for t in range(TILES + 1):
                    if l and t == 0:
                        dve.wait_ge(s_mpar, 16 * 3 * (l + 1))
                        shift_scale(l, 0)
                    if l and t < LAYER_T[l - 1]:
                        combine(l - 1, t)
                    if t:
                        invert_rms(l, 0, t - 1)
                if l == 0:
                    dve.wait_ge(s_mpar, 16 * 3)
                    shift_scale(l, 0)
                shift_scale(l, 1)
                bank = take(dve, l, "vec")
                ins = dve.tensor_copy(chv[:, :, :], bank[:, 0:2 * VEC_ROWS].rearrange("p (m v) -> p m v", m=2))
                done(ins, "D", l, "vec")
                got(dve, "D", l, "vec")
                dve.tensor_copy(wrt[:, :, 0:NE], wre[:, :, :])
                dve.tensor_copy(wrt[:, :, NE:], wrg[:, :, :])
                dve.wait_ge(s_modv, 2 * l + 1)
                modulate(l, 0, TILES)
                for m in range(2):
                    bank = take(dve, l, "ca", m)
                    got(dve, "A", l, "cgate", m)
                    ins = tt(glu[:, m, 0:N], bank[:, 0:N], sg[:, m, 0:N], ALU.mult)
                    done(ins, "D", l, "ca", m)
                got(dve, "D", l, "ca", 1)
                chains = []
                for m in range(2):
                    chains += taps(u, glu, m, 0, CONF_K, nt == TILES, chv[:, m, V_CB:V_CB + 1])
                run_chains(chains)
                dve.sem_inc(s_u, 1)
                for m in range(2):
                    bank = take(dve, l, "scx", m)
                    got(dve, "A", l, "scc", m)
                    ins = tt(scp[:, m, 0:N], bank[:, 0:N], scc[:, m, 0:N], ALU.mult)
                    done(ins, "D", l, "scx", m)
                got(dve, "D", l, "scx", 1)
                chains = []
                for m in range(2):
                    chains += taps(sca, scp, m, V_SC, SC_K, nt == TILES, None)
                run_chains(chains)
                for m in range(2):
                    tt(sca[:, m, 0:N], sca[:, m, 0:N], scb[:, m, 0:N], ALU.mult)
                dve.wait_ge(s_lab, l + 1)
                for i in range(2):
                    bank = take(dve, l, "zw", i)
                    for d in range(2):
                        z = bank[:, :].rearrange("p (t d c) -> p d t c", t=2, d=2)[:, d, :, :]
                        ins = stt(la[:, d, 2 * i:2 * i + 2, :], z, 0.0, lab[:, d, 2 * i:2 * i + 2, :], ALU.min,
                                  ALU.subtract)
                    done(ins, "D", l, "zw", i)
                bank = take(dve, l, "mean")
                for m in range(2):
                    ins = stt(glu[:, m, 0:N], bank[:, 0:N], -1.0 / GROUP_W, u[:, m, 0:N], ALU.mult, ALU.add)
                done(ins, "D", l, "mean")
                got(dve, "A", l, "var")
                r = u[:, 0, 0:N]
                link(dve.reciprocal(r, r))
                for m in range(2):
                    ins = tt(glu[:, m, 0:N], glu[:, m, 0:N], r, ALU.mult)
                ins.then_inc(s_un, 1)
                dve.wait_ge(s_un, l + 1)
                for m in range(2):
                    bank = take(dve, l, "pm", m)
                    done(ts(u[:, m, 0:N], bank[:, 0:N], chv[:, m, V_PS:V_PS + 1], None, ALU.mult),
                         "D", l, "pm", m)
                got(dve, "A", l, "qkv", TILES - 1)
                for d in range(2):
                    got(dve, "A", l, "cum", 2 * d + 1)
                    q = qkvg[:, :, 0:QK_W]
                    k = qkvg[:, :, QK_W:2 * QK_W]
                    qt = TILES if nt == TILES else nt
                    stt(ex[:, 3 * d, 0:qt, :], q[:, 0:qt, :], DK ** -0.5, ex[:, 3 * d, 0:qt, :], ALU.mult, ALU.mult)
                    tt(ex[:, 3 * d + 1, :, :], k, ex[:, 3 * d + 1, :, :], ALU.mult)
                    tt(ex[:, 3 * d + 2, :, :], k, ex[:, 3 * d + 2, :, :], ALU.mult).then_inc(s_qd, 1)
                shift_scale(l, 2)
                heads = const("heads")
                got(dve, "A", l, "dec")
                for t in (2, 3, 0, 1):
                    for par in range(2):
                        c = 2 * t + par
                        bank = take(dve, l, "kv", t, par)
                        for d in range(2):
                            ins = tt(S[:, d, c, :].rearrange("p (h v) -> p h v", h=HEADS),
                                     bank[:, 256 * d:256 * d + 256].rearrange("p (h v) -> p h v", h=HEADS),
                                     bc(heads, 2, DV), ALU.mult)
                        done(ins, "D", l, "kv", t, par)
                got(dve, "D", l, "kv", 1, 1)
                def masked(t):
                    for d in range(2):
                        bank = take(dve, l, "score", t, d)
                        mask = bc(const("cum_b" if d else "cum_f"), 1, HEADS)
                        ins = tt(scm[:, d, :].rearrange("p (h i) -> p h i", h=HEADS),
                                 bank[:, :].rearrange("p (h i) -> p h i", h=HEADS), mask, ALU.mult)
                        done(ins, "D", l, "score", t, d)

                masked(0)
                for n in range(1, NCH):
                    for d in range(2):
                        c, p = ORDER[d][n], ORDER[d][n - 1]
                        v = step(stt(S[:, d, c, :], S[:, d, p, :], dec[:, d, c:c + 1], S[:, d, c, :], ALU.mult, ALU.add))
                    dve.wait_ge(s_dve, v)
                dve.sem_inc(s_S, 1)

                def rows(t):
                    bank = take(dve, l, "o", t)
                    if t + 1 < nt:
                        masked(t + 1)
                    got(dve, "A", l, "g", t)
                    g = qkvg[:, t, 512:768]
                    link(tt(g, g, gout[:, :], ALU.mult))
                    got(dve, "A", l, "o", t)
                    sq = ex[:, t % 2, 0:2, :].rearrange("p t c -> p (t c)").rearrange("p (h v) -> p h v", h=HEADS)
                    so = sso[:, HEADS * t:HEADS * (t + 1)]
                    dve.tensor_reduce(so, sq, AX_X, ALU.add).then_inc(s_so, 1)
                    rh = ro[:, HEADS * t:HEADS * (t + 1)]
                    dve.wait_ge(s_ro, n_y + t + 1)
                    link(dve.reciprocal(rh, so))
                    ins = tt(sq, bank[:, 0:256].rearrange("p (h v) -> p h v", h=HEADS), bc(rh, 2, DV), ALU.mult)
                    done(ins, "D", l, "o", t)
                    got(dve, "D", l, "o", t)
                    tt(g, sq.rearrange("p h v -> p (h v)"), g, ALU.mult).then_inc(s_y, 1)

                def residual(t, h):
                    if t == h == 0:
                        dve.wait_ge(s_gb, 16 * GATE_LOADS[l, 2])
                    elif h and t == nt - 1:
                        for before in range(t):
                            invert_rms(l, 1, before)
                    bank = take(dve, l, "out", t, h)
                    tmp = ex[:, 2 + h, :, :].rearrange("p t c -> p (t c)")
                    c = slice(512 * h, 512 * h + 512)
                    ins = tt(tmp, bank[:, :], gates[:, t // XT_TILES, c], ALU.mult)
                    done(ins, "D", l, "out", t, h)
                    got(dve, "D", l, "out", t, h)
                    ins = tt(X[:, t, c], X[:, t, c], tmp, ALU.add)
                    if h:
                        ins.then_inc(s_res, 1)

                order = [k for k in gla_steps(l) if k[0] in ("o", "out", "modT")]
                stages = {"o": rows, "out": residual, "modT": lambda i: shift_scale(l, i)}
                for name, *args in order:
                    stages[name](*args)
                invert_rms(l, 1, nt - 1)
                dve.wait_ge(s_modv, 2 * l + 2)
                modulate(l, 1, nt)
                route(dve, link, tt, ts, stt, shift_scale, l, nt)
                m0 = (NE + 1) * l
                dve.sem_inc(m_y, 1)

                def tokens(bank, x, ms, value, up):
                    dve.wait_ge(ms, value)
                    dve.tensor_copy(x, bank[:, :].rearrange("p (k n) -> p k n", k=4)).then_inc(up, 1)

                def act_rows(bank, s, h_, ms, value, up):
                    dve.wait_ge(ms, value)
                    tt(h_, s, bank[:, :].rearrange("p (k n) -> p k n", k=4)[:, :, BLK:2 * BLK], ALU.mult).then_inc(up, 1)

                def out_rows(bank, y, ms, value, up):
                    dve.wait_ge(ms, value)
                    dve.tensor_copy(y, bank[:, :]).then_inc(up, 1)

                tokens(PS[0], xeT[:, 0, :, :], m_t1, m0 + 1, m_xeT)
                with dve.Fori(0, NE // BUFS) as turn:
                    e0 = turn * BUFS
                    for i in range(BUFS):
                        par = i % 2
                        n = NE * l + i + 1
                        tokens(PS[0], xeT[:, 1 - par, :, :], m_t1, e0 + (m0 + i + 2), m_xeT)
                        act_rows(PS[2], sil, hT, m_sil, e0 + n, m_hT)
                        dve.wait_ge(m_scat[i], turn * 16 + (16 * ((NE // BUFS) * l + 1)))
                        out_rows(PS[3], ye[:, i, :], m_g2, e0 + n, m_y)
                        n_x = dve.value_load(xtab[0:1, bass.ds(e0 + (NE + i), 1)], min_val=0, max_val=7)
                        k0 = dve.value_load(xtab[0:1, bass.ds(e0 + i, 1)], min_val=0, max_val=16)
                        with dve.If(n_x > 0):
                            with dve.Fori(0, n_x) as b:
                                k = k0 + b
                                tokens(PS[4], xeT_x, x_t1[l], k + 1, x_xeT[l])
                                act_rows(PS[6], sil_x, hT_x, x_sil[l], k + 1, x_hT[l])
                                out_rows(PS[7], ye_x, x_g2[l], k + 1, x_y[l])
            for t in range(XT_TILES + 1):
                if t < XT_TILES:
                    combine(DEPTH - 1, t)
                if t:
                    invert_rms(DEPTH, 0, t - 1)
            dve.wait_ge(s_rstd, norm_base(DEPTH, 0) + XT_TILES)
            dve.wait_ge(s_gf, 16)
            for t in range(XT_TILES):
                stt(X[:, t, :], X[:, t, :], rstd[:, t:t + 1], gfin, ALU.mult, ALU.mult).then_inc(s_fin, 1)


_INS = ['x', 'c', 'ctx', 'c_ctx', 'w_mod', 'b_mod', 'g_norm1', 'g_norm2', 'w_in', 'gla_w_gate_f', 'gla_b_gate_f',
        'gla_w_gate_b', 'gla_b_gate_b', 'gla_g_out', 'conf_w_dw', 'conf_b_dw', 'conf_ln_g', 'conf_ln_b', 'sc_w_dw',
        'pool_w', 'pool_scale', 'w_out', 'router_w_group', 'router_b_group', 'router_w_expert', 'router_b_expert',
        'expert_w_in', 'expert_w_out', 'g_final']


def kernel(**inputs):
    import numpy as _np
    import concourse.bacc as _bacc
    from concourse import mybir as _mybir
    from concourse.bass_utils import run_bass_kernel_spmd as _run

    nc = _bacc.Bacc("TRN2", target_bir_lowering=False, num_devices=1)
    arrays, args = {}, {}
    for name in _INS:
        a = _np.ascontiguousarray(inputs[name])
        arrays[f"in_{name}"] = a
        args[name] = nc.dram_tensor(f"in_{name}", a.shape, _mybir.dt.from_np(a.dtype), kind="ExternalInput").ap()
    arrays["in_consts"] = constants()
    args["consts"] = nc.dram_tensor("in_consts", (P, CONST_N), F32, kind="ExternalInput").ap()
    o = nc.dram_tensor("out_0", (1, SEQ, D), F32, kind="ExternalOutput").ap()
    build(nc, args, o)
    r = _run(nc, [arrays], core_ids=[0])
    return r.results[0]["out_0"]
```
